# Optimizing a Trainium2 kernel written in Bass

```python
import math
import jax
import jax.numpy as jnp
from jax import lax
import numpy as np

D_MODEL = 1024
BATCH = 1
SEQ = 1024
DEPTH = 2

GROUP_W = D_MODEL // 4
SSM_HEADS = 4
SSM_HEAD_DIM = GROUP_W // SSM_HEADS
SSM_GROUPS = 2
SSM_STATE = 128
SSM_CONV = 4
SSM_CHUNK = 128
SSM_XBC = GROUP_W + 2 * SSM_GROUPS * SSM_STATE
MLA_HEADS = 4
MLA_NOPE = 64
MLA_ROPE = 32
MLA_V = GROUP_W // MLA_HEADS
MLA_Q_RANK = 256
MLA_KV_RANK = 128
RET_HEADS = 4
RET_DK = 64
RET_DV = GROUP_W // RET_HEADS
RET_CHUNK = 128
NSA_HEADS = 4
NSA_DK = 64
NSA_DV = GROUP_W // NSA_HEADS
NSA_CMP_LEN = 32
NSA_CMP_STRIDE = 16
NSA_CMP_HID = 256
NSA_SLC_LEN = 64
NSA_TOPN = 16
NSA_WIN = 512
D_FF = 4 * D_MODEL
Q_BLOCK = 128
ROPE_THETA = 10000.0
EPS = 1e-5
NEG_INF = -1e30
FORCED_SCORE = 1e9
DEEPNORM_ALPHA = (2.0 * DEPTH) ** 0.25
DEEPNORM_BETA = (8.0 * DEPTH) ** -0.25

IN_SPLITS = (
    GROUP_W, SSM_XBC, SSM_HEADS,
    MLA_Q_RANK, MLA_KV_RANK, MLA_ROPE,
    RET_HEADS * RET_DK, RET_HEADS * RET_DK, RET_HEADS * RET_DV, GROUP_W,
    NSA_HEADS * NSA_DK, NSA_DK, NSA_DV, NSA_DK, NSA_DV, NSA_DK, NSA_DV, 3 * NSA_HEADS,
)
D_IN = sum(IN_SPLITS)

kernel_name = 'hybrid_ssd_mla_retention_nsa'

def split_columns(proj):
    offsets = [int(o) for o in np.cumsum(IN_SPLITS)[:-1]]
    return jnp.split(proj, offsets, axis=-1)

def layer_norm(x, g, b):
    xf = x.astype(jnp.float32)
    mu = jnp.mean(xf, axis=-1, keepdims=True)
    var = jnp.mean(jnp.square(xf - mu), axis=-1, keepdims=True)
    return ((xf - mu) * lax.rsqrt(var + EPS)).astype(x.dtype) * g + b

def rms_norm(x, g=None):
    xf = x.astype(jnp.float32)
    y = (xf * lax.rsqrt(jnp.mean(xf * xf, axis=-1, keepdims=True) + EPS)).astype(x.dtype)
    return y if g is None else y * g

def rope_tables(seq, dim):
    inv = ROPE_THETA ** (-jnp.arange(0, dim, 2, dtype=jnp.float32) / dim)
    ang = jnp.arange(seq, dtype=jnp.float32)[:, None] * inv[None, :]
    return jnp.cos(ang), jnp.sin(ang)

def apply_rope(x, cos, sin):
    x1, x2 = jnp.split(x, 2, axis=-1)
    c = cos[:, None, :].astype(x.dtype)
    s = sin[:, None, :].astype(x.dtype)
    return jnp.concatenate([x1 * c - x2 * s, x1 * s + x2 * c], axis=-1)

def causal_block_attention(q, k, v):
    bsz, S, H, D = q.shape
    nb = S // Q_BLOCK
    q_b = jnp.moveaxis(q.reshape(bsz, nb, Q_BLOCK, H, D), 1, 0)
    kpos = jnp.arange(S)

    def one_block(args):
        i, qi = args
        qpos = i * Q_BLOCK + jnp.arange(Q_BLOCK)
        s = jnp.einsum('bqhd,bkhd->bhqk', qi, k).astype(jnp.float32)
        s = jnp.where(kpos[None, :] <= qpos[:, None], s, NEG_INF)
        p = jax.nn.softmax(s, axis=-1).astype(v.dtype)
        return jnp.einsum('bhqk,bkhd->bqhd', p, v)

    out = lax.map(one_block, (jnp.arange(nb), q_b))
    return jnp.moveaxis(out, 0, 1).reshape(bsz, S, H, v.shape[-1])

def causal_depthwise_conv(u, w, b):
    y = lax.conv_general_dilated(u, w[:, None, :], window_strides=(1,), padding=[(SSM_CONV - 1, 0)],
                                 dimension_numbers=('NWC', 'WIO', 'NWC'), feature_group_count=u.shape[-1])
    return y + b

def segsum_exp(a):
    T = a.shape[-1]
    cs = jnp.cumsum(a, axis=-1)
    diff = cs[..., :, None] - cs[..., None, :]
    mask = jnp.tril(jnp.ones((T, T), dtype=bool))
    return jnp.where(mask, jnp.exp(jnp.where(mask, diff, 0.0)), 0.0)

def mamba2_ssd(z, xbc, dt_raw, conv_w, conv_b, dt_bias, a_log, d_skip, norm_g):
    bsz, S, _ = z.shape
    H, P, N, L = SSM_HEADS, SSM_HEAD_DIM, SSM_STATE, SSM_CHUNK
    nc = S // L
    xbc = jax.nn.silu(causal_depthwise_conv(xbc, conv_w, conv_b))
    xs, b_in, c_in = jnp.split(xbc, [GROUP_W, GROUP_W + SSM_GROUPS * N], axis=-1)
    xs = xs.reshape(bsz, S, H, P)
    rep = H // SSM_GROUPS
    b_h = jnp.repeat(b_in.reshape(bsz, S, SSM_GROUPS, N), rep, axis=2)
    c_h = jnp.repeat(c_in.reshape(bsz, S, SSM_GROUPS, N), rep, axis=2)
    dt = jax.nn.softplus(dt_raw + dt_bias)
    a = jnp.moveaxis((dt * -jnp.exp(a_log)).reshape(bsz, nc, L, H), 3, 1)
    xdt = (xs * dt[..., None]).reshape(bsz, nc, L, H, P)
    bc = b_h.reshape(bsz, nc, L, H, N)
    cc = c_h.reshape(bsz, nc, L, H, N)
    a_cs = jnp.cumsum(a, axis=-1)
    scores = jnp.einsum('bclhn,bcshn->bhcls', cc, bc) * segsum_exp(a)
    y_diag = jnp.einsum('bhcls,bcshp->bclhp', scores, xdt)
    decay_to_end = jnp.exp(a_cs[..., -1:] - a_cs)
    states = jnp.einsum('bclhn,bhcl,bclhp->bchpn', bc, decay_to_end, xdt)
    chunk_decay = jnp.exp(a_cs[..., -1])

    def step(h_state, inp):
        st, dec = inp
        return h_state * dec[..., None, None] + st, h_state

    _, prev = lax.scan(step, jnp.zeros_like(states[:, 0]),
                       (jnp.moveaxis(states, 1, 0), jnp.moveaxis(chunk_decay, 2, 0)))
    prev = jnp.moveaxis(prev, 0, 1)
    y_off = jnp.einsum('bclhn,bchpn,bhcl->bclhp', cc, prev, jnp.exp(a_cs))
    y = (y_diag + y_off).reshape(bsz, S, H, P) + xs * d_skip[:, None]
    y = y.reshape(bsz, S, GROUP_W) * jax.nn.silu(z)
    return rms_norm(y, norm_g)

def mla(c_q, c_kv, k_rope, q_norm_g, w_uq, kv_norm_g, w_ukv, cos, sin):
    bsz, S, _ = c_q.shape
    H = MLA_HEADS
    q = (rms_norm(c_q, q_norm_g) @ w_uq).reshape(bsz, S, H, MLA_NOPE + MLA_ROPE)
    q_nope, q_pe = jnp.split(q, [MLA_NOPE], axis=-1)
    q = jnp.concatenate([q_nope, apply_rope(q_pe, cos, sin)], axis=-1) * ((MLA_NOPE + MLA_ROPE) ** -0.5)
    kv = (rms_norm(c_kv, kv_norm_g) @ w_ukv).reshape(bsz, S, H, MLA_NOPE + MLA_V)
    k_nope, v = jnp.split(kv, [MLA_NOPE], axis=-1)
    k_pe = jnp.broadcast_to(apply_rope(k_rope[:, :, None, :], cos, sin), (bsz, S, H, MLA_ROPE))
    k = jnp.concatenate([k_nope, k_pe], axis=-1)
    return causal_block_attention(q, k, v).reshape(bsz, S, GROUP_W)

def retention(q, k, v, gate, cos, sin):
    bsz, S, _ = q.shape
    H, dk, dv, L = RET_HEADS, RET_DK, RET_DV, RET_CHUNK
    nc = S // L
    dt = q.dtype
    q = apply_rope(q.reshape(bsz, S, H, dk), cos, sin)
    k = apply_rope(k.reshape(bsz, S, H, dk), cos, sin) * (dk ** -0.5)
    qc = q.reshape(bsz, nc, L, H, dk)
    kc = k.reshape(bsz, nc, L, H, dk)
    vc = v.reshape(bsz, nc, L, H, dv)
    log_gamma = jnp.log1p(-jnp.exp2(-5.0 - jnp.arange(H, dtype=jnp.float32)))
    pos = jnp.arange(L, dtype=jnp.float32)
    diff = pos[:, None] - pos[None, :]
    decay_in = jnp.where(diff >= 0, jnp.exp(jnp.maximum(diff, 0.0)[None] * log_gamma[:, None, None]), 0.0).astype(dt)
    zeta = jnp.exp((L - 1 - pos)[None] * log_gamma[:, None]).astype(dt)
    xi = jnp.exp((pos + 1.0)[None] * log_gamma[:, None]).astype(dt)
    chunk_decay = jnp.exp(L * log_gamma).astype(dt)
    scores = jnp.einsum('bclhd,bcshd->bhcls', qc, kc) * decay_in[None, :, None]
    y_in = jnp.einsum('bhcls,bcshv->bclhv', scores, vc)
    kv = jnp.einsum('bclhd,hl,bclhv->bchdv', kc, zeta, vc)

    def step(state, kv_c):
        return state * chunk_decay[None, :, None, None] + kv_c, state

    _, prev = lax.scan(step, jnp.zeros_like(kv[:, 0]), jnp.moveaxis(kv, 1, 0))
    prev = jnp.moveaxis(prev, 0, 1)
    y_cross = jnp.einsum('bclhd,hl,bchdv->bclhv', qc, xi, prev)
    y = rms_norm((y_in + y_cross).reshape(bsz, S, H, dv))
    return y.reshape(bsz, S, GROUP_W) * jax.nn.silu(gate)

def nsa(q, k_cmp_raw, v_cmp_raw, k_slc, v_slc, k_win, v_win, gate_logits,
        pe_k, w1_k, w2_k, pe_v, w1_v, w2_v):
    bsz, S, _ = q.shape
    H, dk, dv = NSA_HEADS, NSA_DK, NSA_DV
    f32 = jnp.float32
    q = q.reshape(bsz, S, H, dk) * (dk ** -0.5)
    gates = jax.nn.sigmoid(gate_logits.reshape(bsz, S, H, 3))
    slopes = jnp.exp2(-8.0 * jnp.arange(1, H + 1, dtype=f32) / H)
    n_cmp = (S - NSA_CMP_LEN) // NSA_CMP_STRIDE + 1
    cmp_start = jnp.arange(n_cmp) * NSA_CMP_STRIDE
    cmp_tok = cmp_start[:, None] + jnp.arange(NSA_CMP_LEN)[None, :]
    cmp_end = cmp_start + NSA_CMP_LEN - 1
    cmp_center = cmp_start.astype(f32) + 0.5 * (NSA_CMP_LEN - 1)

    def compress(u, pe, w1, w2):
        blocks = (u[:, cmp_tok] + pe).reshape(bsz, n_cmp, NSA_CMP_LEN * u.shape[-1])
        return jax.nn.silu(blocks @ w1) @ w2

    k_cmp = compress(k_cmp_raw, pe_k, w1_k, w2_k)
    v_cmp = compress(v_cmp_raw, pe_v, w1_v, w2_v)
    n_slc = S // NSA_SLC_LEN
    top_n = min(NSA_TOPN, n_slc)
    slc_start = jnp.arange(n_slc) * NSA_SLC_LEN
    overlap = ((cmp_start[:, None] < slc_start[None, :] + NSA_SLC_LEN)
               & (cmp_end[:, None] >= slc_start[None, :])).astype(f32)
    k_blocks = k_slc.reshape(bsz, n_slc, NSA_SLC_LEN, dk)
    v_blocks = v_slc.reshape(bsz, n_slc, NSA_SLC_LEN, dv)
    bidx = jnp.arange(bsz)[:, None, None]
    k_win_pad = jnp.pad(k_win, ((0, 0), (NSA_WIN, 0), (0, 0)))
    v_win_pad = jnp.pad(v_win, ((0, 0), (NSA_WIN, 0), (0, 0)))
    nb = S // Q_BLOCK
    q_b = jnp.moveaxis(q.reshape(bsz, nb, Q_BLOCK, H, dk), 1, 0)
    g_b = jnp.moveaxis(gates.reshape(bsz, nb, Q_BLOCK, H, 3), 1, 0)

    def one_block(args):
        i, qi, gi = args
        qpos = i * Q_BLOCK + jnp.arange(Q_BLOCK)
        qpos_f = qpos.astype(f32)
        valid_c = cmp_end[None, :] <= qpos[:, None]
        s_c = (jnp.einsum('bqhd,bnd->bhqn', qi, k_cmp).astype(f32)
               - slopes[:, None, None] * (qpos_f[:, None] - cmp_center[None, :]))
        s_c = jnp.where(valid_c, s_c, NEG_INF)
        p_c = jax.nn.softmax(s_c, axis=-1) * jnp.any(valid_c, axis=-1)[:, None].astype(f32)
        o_c = jnp.einsum('bhqn,bnd->bqhd', p_c.astype(v_cmp.dtype), v_cmp)
        imp = jnp.einsum('bhqn,nj->bqj', p_c, overlap)
        blk = jnp.arange(n_slc)
        q_blk = qpos // NSA_SLC_LEN
        causal_blk = slc_start[None, :] <= qpos[:, None]
        forced = (blk[None, :] == 0) | (blk[None, :] == q_blk[:, None]) | (blk[None, :] == q_blk[:, None] - 1)
        imp = jnp.where(forced & causal_blk, FORCED_SCORE, imp)
        imp = jnp.where(causal_blk, imp, -1.0)
        _, sel = lax.top_k(imp, top_n)
        k_sel = k_blocks[bidx, sel].reshape(bsz, Q_BLOCK, top_n * NSA_SLC_LEN, dk)
        v_sel = v_blocks[bidx, sel].reshape(bsz, Q_BLOCK, top_n * NSA_SLC_LEN, dv)
        pos_sel = (sel[..., None] * NSA_SLC_LEN + jnp.arange(NSA_SLC_LEN)).reshape(bsz, Q_BLOCK, -1)
        dist_s = (qpos[None, :, None] - pos_sel).astype(f32)
        s_s = (jnp.einsum('bqhd,bqkd->bhqk', qi, k_sel).astype(f32)
               - slopes[None, :, None, None] * dist_s[:, None])
        s_s = jnp.where((dist_s >= 0)[:, None], s_s, NEG_INF)
        p_s = jax.nn.softmax(s_s, axis=-1).astype(v_sel.dtype)
        o_s = jnp.einsum('bhqk,bqkd->bqhd', p_s, v_sel)
        k_w = lax.dynamic_slice_in_dim(k_win_pad, i * Q_BLOCK, Q_BLOCK + NSA_WIN, axis=1)
        v_w = lax.dynamic_slice_in_dim(v_win_pad, i * Q_BLOCK, Q_BLOCK + NSA_WIN, axis=1)
        kpos = i * Q_BLOCK - NSA_WIN + jnp.arange(Q_BLOCK + NSA_WIN)
        dist_w = qpos[:, None] - kpos[None, :]
        valid_w = (dist_w >= 0) & (dist_w < NSA_WIN) & (kpos[None, :] >= 0)
        s_w = (jnp.einsum('bqhd,bkd->bhqk', qi, k_w).astype(f32)
               - slopes[:, None, None] * dist_w.astype(f32))
        s_w = jnp.where(valid_w, s_w, NEG_INF)
        p_w = jax.nn.softmax(s_w, axis=-1).astype(v_w.dtype)
        o_w = jnp.einsum('bhqk,bkd->bqhd', p_w, v_w)
        return gi[..., 0:1] * o_c + gi[..., 1:2] * o_s + gi[..., 2:3] * o_w

    out = lax.map(one_block, (jnp.arange(nb), q_b, g_b))
    return jnp.moveaxis(out, 0, 1).reshape(bsz, S, GROUP_W)

def setup_inputs(seed: int = 0) -> dict:
    key = jax.random.key(seed)
    ks = jax.random.split(key, 32)
    f32 = jnp.float32
    L = DEPTH

    def nrm(k, shape, fan_in, scale=1.0):
        return jax.random.normal(k, shape, f32) * (scale * fan_in ** -0.5)

    def gain(k, shape):
        return 1.0 + 0.02 * jax.random.normal(k, shape, f32)

    def small(k, shape):
        return 0.02 * jax.random.normal(k, shape, f32)

    x = jax.random.normal(ks[0], (BATCH, SEQ, D_MODEL), f32)
    dt0 = jnp.exp(jax.random.uniform(ks[6], (L, SSM_HEADS), f32, math.log(1e-3), math.log(1e-1)))
    return {
        'x': x,
        'ln_emb_g': gain(ks[1], (D_MODEL,)),
        'ln_emb_b': small(ks[2], (D_MODEL,)),
        'w_in': nrm(ks[3], (L, D_MODEL, D_IN), D_MODEL),
        'conv_w': nrm(ks[4], (L, SSM_CONV, SSM_XBC), SSM_CONV),
        'conv_b': small(ks[5], (L, SSM_XBC)),
        'dt_bias': dt0 + jnp.log(-jnp.expm1(-dt0)),
        'a_log': jnp.log(jax.random.uniform(ks[7], (L, SSM_HEADS), f32, 1.0, 16.0)),
        'd_skip': gain(ks[8], (L, SSM_HEADS)),
        'ssm_norm_g': gain(ks[9], (L, GROUP_W)),
        'q_norm_g': gain(ks[10], (L, MLA_Q_RANK)),
        'w_uq': nrm(ks[11], (L, MLA_Q_RANK, MLA_HEADS * (MLA_NOPE + MLA_ROPE)), MLA_Q_RANK),
        'kv_norm_g': gain(ks[12], (L, MLA_KV_RANK)),
        'w_ukv': nrm(ks[13], (L, MLA_KV_RANK, MLA_HEADS * (MLA_NOPE + MLA_V)), MLA_KV_RANK),
        'cmp_pe_k': small(ks[14], (L, NSA_CMP_LEN, NSA_DK)),
        'cmp_w1_k': nrm(ks[15], (L, NSA_CMP_LEN * NSA_DK, NSA_CMP_HID), NSA_CMP_LEN * NSA_DK),
        'cmp_w2_k': nrm(ks[16], (L, NSA_CMP_HID, NSA_DK), NSA_CMP_HID),
        'cmp_pe_v': small(ks[17], (L, NSA_CMP_LEN, NSA_DV)),
        'cmp_w1_v': nrm(ks[18], (L, NSA_CMP_LEN * NSA_DV, NSA_CMP_HID), NSA_CMP_LEN * NSA_DV),
        'cmp_w2_v': nrm(ks[19], (L, NSA_CMP_HID, NSA_DV), NSA_CMP_HID),
        'w_out': nrm(ks[20], (L, D_MODEL, D_MODEL), D_MODEL, DEEPNORM_BETA),
        'ln1_g': gain(ks[21], (L, D_MODEL)),
        'ln1_b': small(ks[22], (L, D_MODEL)),
        'w_mlp1': nrm(ks[23], (L, D_MODEL, D_FF), D_MODEL),
        'w_mlp2': nrm(ks[24], (L, D_FF, D_MODEL), D_FF, DEEPNORM_BETA),
        'ln2_g': gain(ks[25], (L, D_MODEL)),
        'ln2_b': small(ks[26], (L, D_MODEL)),
    }

def reference(x, ln_emb_g, ln_emb_b, w_in, conv_w, conv_b, dt_bias, a_log, d_skip, ssm_norm_g,
              q_norm_g, w_uq, kv_norm_g, w_ukv, cmp_pe_k, cmp_w1_k, cmp_w2_k, cmp_pe_v, cmp_w1_v,
              cmp_w2_v, w_out, ln1_g, ln1_b, w_mlp1, w_mlp2, ln2_g, ln2_b):
    S = x.shape[1]
    cos_m, sin_m = rope_tables(S, MLA_ROPE)
    cos_r, sin_r = rope_tables(S, RET_DK)
    h = layer_norm(x, ln_emb_g, ln_emb_b)
    for l in range(DEPTH):
        (ssm_z, ssm_xbc, ssm_dt, mla_cq, mla_ckv, mla_kr, ret_q, ret_k, ret_v, ret_g,
         nsa_q, nsa_kc, nsa_vc, nsa_ks, nsa_vs, nsa_kw, nsa_vw, nsa_gate) = split_columns(h @ w_in[l])
        y_a = mamba2_ssd(ssm_z, ssm_xbc, ssm_dt, conv_w[l], conv_b[l], dt_bias[l], a_log[l], d_skip[l], ssm_norm_g[l])
        y_b = mla(mla_cq, mla_ckv, mla_kr, q_norm_g[l], w_uq[l], kv_norm_g[l], w_ukv[l], cos_m, sin_m)
        y_c = retention(ret_q, ret_k, ret_v, ret_g, cos_r, sin_r)
        y_d = nsa(nsa_q, nsa_kc, nsa_vc, nsa_ks, nsa_vs, nsa_kw, nsa_vw, nsa_gate,
                  cmp_pe_k[l], cmp_w1_k[l], cmp_w2_k[l], cmp_pe_v[l], cmp_w1_v[l], cmp_w2_v[l])
        mix = jnp.concatenate([y_a, y_b, y_c, y_d], axis=-1) @ w_out[l]
        h = layer_norm(DEEPNORM_ALPHA * h + mix, ln1_g[l], ln1_b[l])
        ff = jnp.square(jax.nn.relu(h @ w_mlp1[l])) @ w_mlp2[l]
        h = layer_norm(DEEPNORM_ALPHA * h + ff, ln2_g[l], ln2_b[l])
    return h


_drawn_inputs = setup_inputs


def setup_inputs(seed=0):
    import zlib

    import numpy as np

    out = dict(_drawn_inputs(seed))
    spreads = {}
    factors = {'conv_b': 6.795,
     'd_skip': 8.0,
     'ssm_norm_g': 8.0,
     'q_norm_g': 8.0,
     'kv_norm_g': 8.0,
     'cmp_pe_k': 8.0,
     'cmp_w1_k': 4.696,
     'cmp_w2_k': 4.658,
     'cmp_pe_v': 8.0}
    for name, (base, spread) in spreads.items():
        noise = np.random.default_rng([zlib.crc32(name.encode()), seed]).standard_normal(out[name].shape)
        drawn = base * np.exp(spread * noise) if base else spread * noise
        out[name] = jnp.asarray(drawn.astype(out[name].dtype))
    for name, factor in factors.items():
        out[name] = (out[name] * factor).astype(out[name].dtype)
    return out
```

```python
from collections import namedtuple
from contextlib import ExitStack, contextmanager

import numpy as np

import concourse.bass as bass
from concourse import mybir

F32 = mybir.dt.float32
F32R = mybir.dt.float32r
ACT = mybir.ActivationFunctionType
ALU = mybir.AluOpType
AX = mybir.AxisListType

P = 128
D = 1024
T = 1024
DEPTH = 2
NT = T // P
KT = D // P
GW = D // 4
H = 4
HD = GW // H
STATE = 128
XBC = GW + 2 * 2 * STATE
CONV = 4
QR, KVR, ROPE, NOPE = 256, 128, 32, 64
QD = NOPE + ROPE
DFF = 4 * D
CMP_LEN, CMP_STRIDE, CMP_HID, WIN = 32, 16, 256, 512
NCMP = (T - CMP_LEN) // CMP_STRIDE + 1
EPS = 1e-5
MASKED = -1e30
ALPHA = (2.0 * DEPTH) ** 0.25
SLOPES = [2.0 ** (-8.0 * (h + 1) / H) for h in range(H)]

SPLITS = dict(z=GW, xbc=XBC, dt=H, cq=QR, ckv=KVR, kr=ROPE, rq=GW, rk=GW, rv=GW, rg=GW,
              nq=GW, kc=HD, vc=HD, ks=HD, vs=HD, kw=HD, vw=HD, gate=3 * H)
COL = dict(zip(SPLITS, np.cumsum([0] + list(SPLITS.values()))[:-1].tolist()))
D_IN = sum(SPLITS.values())
SLOT = 256
NSLOT = D_IN // SLOT
REST = D_IN - NSLOT * SLOT


Item = namedtuple("Item", "q k n slope table v gate out adds")


def shape_tables():
    f = np.float32
    tok = np.arange(T, dtype=f)

    def rope(dim):
        inv = f(10000.0) ** (-np.arange(0, dim, 2, dtype=f) / f(dim))
        ang = (tok[:, None] * inv[None, :]).astype(f)
        return np.concatenate([np.cos(ang), np.sin(ang)], 1).astype(f).reshape(NT, P, dim)

    p = np.arange(P)
    log_gamma = np.log1p(-np.exp2(-5.0 - np.arange(H)))
    diff = (p[None, :] - p[:, None]).astype(np.float64)
    decay = np.where(diff[:, None] >= 0, np.exp(np.maximum(diff, 0)[:, None] * log_gamma[None, :, None]), 0)
    zeta = np.exp((P - 1 - p)[:, None] * log_gamma[None])
    xi = np.exp((p + 1)[:, None] * log_gamma[None])
    scale = HD ** -0.5
    u = np.arange(-(T - P), P)
    dist = p[:, None] - u[None, :]
    far = -MASKED * 2.0 ** 8
    uw = np.arange(-WIN, P)
    dw = p[:, None] - uw[None, :]
    qpos = (np.arange(NT) * P)[None, :, None] + p[:, None, None]
    n = np.arange(NCMP)
    valid = n * CMP_STRIDE + CMP_LEN - 1 <= qpos
    dc = qpos - (n * CMP_STRIDE + 0.5 * (CMP_LEN - 1))
    return {
        "t_ident": np.eye(P, dtype=f),
        "t_upto": (p[:, None] <= p[None, :]).astype(f),
        "t_later": np.where(p[:, None] <= p[None, :], 0, MASKED).astype(f),
        "t_rope_ret": np.ascontiguousarray(rope(HD).transpose(1, 0, 2)),
        "t_rope_mla": np.ascontiguousarray(rope(ROPE).transpose(1, 0, 2)),
        "t_decay": (decay * scale).astype(f),
        "t_zeta": (zeta * scale).astype(f),
        "t_xi": xi.astype(f),
        "t_chunk": np.broadcast_to(np.exp(P * log_gamma), (P, H)).astype(f).copy(),
        "t_causal": np.where(dist >= 0, 0, MASKED).astype(f),
        "t_dist": np.where(dist >= 0, dist, far).astype(f),
        "t_dist_win": np.where((dw >= 0) & (dw < WIN), dw, far).astype(f),
        "t_dist_cmp": np.where(valid, dc, far).astype(f),
        "t_any_cmp": valid.any(-1).astype(f),
    }


@contextmanager
def phase(nc, *names):
    first = min(nc.free_semaphores)
    sems = [nc.alloc_semaphore(n, num=first + i) for i, n in enumerate(names)]
    yield namedtuple("Semaphores", names)(*sems)
    nums = [s.num for s in sems]
    assert max(nums) - min(nums) == len(nums) - 1
    nc.all_engine_barrier(sems_to_clear=range(min(nums), max(nums) + 1))
    for s in sems:
        nc.release_semaphore(s)


def tokens(ap, c0, c1):
    return ap.rearrange("(t p) c -> p t c", p=P)[:, :, c0:c1]


def tokens_at(ap, c0, n):
    return ap.rearrange("(t p) c -> p t c", p=P)[:, :, bass.ds(c0, n)]


def layer_norm(nc, tag, x, gain, bias):
    with ExitStack() as c:
        sb = lambda n, s: c.enter_context(nc.sbuf_tensor(f"{tag}_{n}", s, F32))
        g, b = sb("g", [P, D]), sb("b", [P, D])
        stats, mv = sb("stats", [P, NT, 2, 6]), sb("mv", [P, NT, 2])
        var, rstd, shift, power = sb("var", [P, NT]), sb("rstd", [P, NT]), sb("shift", [P, NT]), sb("power", [P, NT])
        s = c.enter_context(phase(nc, "gains_loaded", "power_set", "stats_ready", "moments_ready", "var_ready",
                                  "rstd_ready", "shift_ready", "centred", "scaled"))
        with nc.Block() as block:
            @block.sync
            def _(sp):
                sp.dma_start(g[:], gain.partition_broadcast(P)).then_inc(s.gains_loaded, 16)
                sp.dma_start(b[:], bias.partition_broadcast(P)).then_inc(s.gains_loaded, 16)

            @block.vector
            def _(dve):
                for t in range(NT):
                    for half in range(2):
                        dve.bn_stats(stats[:, t, half, :], x[:, t, half * 512:(half + 1) * 512]).then_inc(s.stats_ready, 1)
                for t in range(NT):
                    dve.wait_ge(s.stats_ready, 2 * t + 2)
                    dve.bn_aggr(mv[:, t, :], stats[:, t, :, :].rearrange("p a b -> p (a b)")).then_inc(s.moments_ready, 1)
                dve.wait_ge(s.moments_ready, NT)
                dve.tensor_scalar(var[:], mv[:, :, 1], EPS, None, ALU.add).then_inc(s.var_ready, 1)
                dve.wait_ge(s.rstd_ready, 1)
                dve.scalar_tensor_tensor(shift[:], mv[:, :, 0], -1.0, rstd[:], ALU.mult, ALU.mult).then_inc(s.shift_ready, 1)
                dve.wait_ge(s.gains_loaded, 32)
                for t in range(NT):
                    dve.wait_ge(s.centred, t + 1)
                    dve.tensor_tensor(x[:, t, :], x[:, t, :], g[:], ALU.mult).then_inc(s.scaled, 1)

            @block.gpsimd
            def _(pool):
                pool.memset(power[:], -0.5).then_inc(s.power_set, 1)
                pool.wait_ge(s.power_set, 1)
                pool.wait_ge(s.var_ready, 1)
                pool.tensor_tensor(rstd[:], var[:], power[:], ALU.pow).then_inc(s.rstd_ready, 1)
                pool.wait_ge(s.gains_loaded, 32)
                for t in range(NT):
                    pool.wait_ge(s.scaled, t + 1)
                    pool.tensor_tensor(x[:, t, :], x[:, t, :], b[:], ALU.add)

            @block.scalar
            def _(act):
                act.wait_ge(s.shift_ready, 1)
                for t in range(NT):
                    act.activation(x[:, t, :], x[:, t, :], ACT.Identity, bias=shift[:, t:t + 1],
                                   scale=rstd[:, t:t + 1]).then_inc(s.centred, 1)


def feature_major(nc, tag, src, hi, lo, ident):
    with ExitStack() as c:
        turned = c.enter_context(nc.psum_tensor(f"{tag}_turned", [P, 8, 4, P], F32))
        s = c.enter_context(phase(nc, "bank_turned", "hi_copied", "lo_copied"))
        groups = [(t, half) for t in range(NT) for half in range(2)]
        with nc.Block() as block:
            @block.tensor
            def _(pe):
                for g, (t, half) in enumerate(groups):
                    if g >= 8:
                        pe.wait_ge(s.lo_copied, g - 7)
                    for j in range(4):
                        k = 4 * half + j
                        mm = pe.transpose(turned[:, g % 8, j, :], src[:, t, k * P:(k + 1) * P], ident[:])
                    mm.then_inc(s.bank_turned, 1)

            @block.scalar
            def _(act):
                for g, (t, half) in enumerate(groups):
                    act.wait_ge(s.bank_turned, g + 1)
                    act.activation(hi[:, 4 * half:4 * half + 4, t * P:(t + 1) * P], turned[:, g % 8, :, :],
                                   ACT.Copy).then_inc(s.hi_copied, 1)

            @block.vector
            def _(dve):
                for g, (t, half) in enumerate(groups):
                    dve.wait_ge(s.hi_copied, g + 1)
                    dst = slice(4 * half, 4 * half + 4), slice(t * P, (t + 1) * P)
                    dve.tensor_tensor(lo[:, dst[0], dst[1]], turned[:, g % 8, :, :],
                                      hi[:, dst[0], dst[1]].bitcast(F32), ALU.subtract).then_inc(s.lo_copied, 1)


def weight_slot(w, c0, n):
    return w.rearrange("(k p) c -> p k c", p=P)[:, :, bass.ds(c0, n)]


def project(nc, tag, w, cols, hi, lo, to_dram=None, into=None):
    full, rest = cols // SLOT, cols % SLOT
    assert full % 2 == 0
    with ExitStack() as c:
        raw = c.enter_context(nc.sbuf_tensor(f"{tag}_raw", [P, 2, KT, SLOT], F32))
        whi = [c.enter_context(nc.sbuf_tensor(f"{tag}_whi{i}", [P, KT, SLOT], F32R)) for i in range(2)]
        wlo = [c.enter_context(nc.sbuf_tensor(f"{tag}_wlo{i}", [P, KT, SLOT], F32R)) for i in range(2)]
        acc = c.enter_context(nc.psum_tensor(f"{tag}_acc", [P, 8, 512], F32))
        if to_dram is not None:
            stage = c.enter_context(nc.sbuf_tensor(f"{tag}_stage", [P, 2, NT, SLOT], F32))
        s = c.enter_context(phase(nc, "raw_loaded0", "raw_loaded1", "whi_ready", "wlo_ready",
                                  "acc_ready", "acc_free", "stage_full", "stored0", "stored1"))
        loaded, stored = [s.raw_loaded0, s.raw_loaded1], [s.stored0, s.stored1]
        n_slots = full + (1 if rest else 0)

        with nc.Block() as block:
            @block.sync
            def _(sp):
                def load(n, b, width, first=False):
                    if not first:
                        sp.wait_ge(s.wlo_ready, n - 1)
                    sp.dma_start(raw[:, b, :, 0:width], weight_slot(w, n * SLOT, width)).then_inc(loaded[b], 16)

                def store(n, b, width):
                    sp.wait_ge(s.stage_full, n * NT + NT)
                    sp.dma_start(tokens_at(to_dram, n * SLOT, width), stage[:, b, :, 0:width]).then_inc(stored[b], 16)

                load(0, 0, SLOT, first=True)
                load(1, 1, SLOT, first=True)
                with sp.Fori(0, full // 2 - 1) as i:
                    for b in range(2):
                        load(2 * i + b + 2, b, SLOT)
                        if to_dram is not None:
                            store(2 * i + b, b, SLOT)
                if rest:
                    load(full, 0, rest)
                if to_dram is not None:
                    store(full - 2, 0, SLOT)
                    store(full - 1, 1, SLOT)
                    if rest:
                        store(full, 0, rest)
                    sp.wait_ge(stored[0], 16 * ((n_slots + 1) // 2))
                    sp.wait_ge(stored[1], 16 * (n_slots // 2))

            @block.scalar
            def _(act):
                def split_hi(n, b, turn, width, first=False):
                    act.wait_ge(loaded[b], 16 * turn + 16)
                    if not first:
                        act.wait_ge(s.acc_ready, n * NT - NT)
                    act.activation(whi[b][:, :, 0:width], raw[:, b, :, 0:width], ACT.Copy).then_inc(s.whi_ready, 1)

                def copy_out(n, b, turn, width):
                    act.wait_ge(stored[b], 16 * turn)
                    for t in range(NT):
                        act.wait_ge(s.acc_ready, n * NT + t + 1)
                        act.activation(stage[:, b, t, 0:width], acc[:, t, 0:width], ACT.Copy).then_inc(s.stage_full, 1)

                split_hi(0, 0, 0, SLOT, first=True)
                split_hi(1, 1, 0, SLOT, first=True)
                if to_dram is None:
                    for n in range(2, n_slots):
                        split_hi(n, n % 2, n // 2, SLOT)
                    return
                for b in range(2):
                    for t in range(NT):
                        act.wait_ge(s.acc_ready, b * NT + t + 1)
                        act.activation(stage[:, b, t, :], acc[:, t, 0:SLOT], ACT.Copy).then_inc(s.stage_full, 1)
                    split_hi(b + 2, b, 1, SLOT)
                with act.Fori(1, full // 2 - 1) as i:
                    for b in range(2):
                        copy_out(2 * i + b, b, i, SLOT)
                        split_hi(2 * i + b + 2, b, i + 1, SLOT)
                i = full // 2 - 1
                copy_out(full - 2, 0, i, SLOT)
                if rest:
                    split_hi(full, 0, i + 1, rest)
                copy_out(full - 1, 1, i, SLOT)
                if rest:
                    copy_out(full, 0, i + 1, rest)

            @block.vector
            def _(dve):
                def split_lo(n, b, width):
                    dve.wait_ge(s.whi_ready, n + 1)
                    dve.tensor_tensor(wlo[b][:, :, 0:width], raw[:, b, :, 0:width],
                                      whi[b][:, :, 0:width].bitcast(F32), ALU.subtract).then_inc(s.wlo_ready, 1)
                def add_in(n):
                    for t in range(NT):
                        dve.wait_ge(s.acc_ready, n * NT + t + 1)
                        here = into[:, t, n * SLOT:(n + 1) * SLOT]
                        dve.scalar_tensor_tensor(here, here, ALPHA, acc[:, t, 0:SLOT], ALU.mult,
                                                 ALU.add).then_inc(s.acc_free, 1)

                split_lo(0, 0, SLOT)
                if to_dram is None:
                    for n in range(n_slots):
                        if n + 1 < n_slots:
                            split_lo(n + 1, (n + 1) % 2, SLOT)
                        add_in(n)
                    return
                split_lo(1, 1, SLOT)
                with dve.Fori(1, full // 2) as i:
                    for b in range(2):
                        split_lo(2 * i + b, b, SLOT)
                if rest:
                    split_lo(full, 0, rest)

            @block.tensor
            def _(pe):
                free = s.acc_free if to_dram is None else s.stage_full

                def slot(n, b, width, first=False):
                    pe.wait_ge(s.wlo_ready, n + 1)
                    for t in range(NT):
                        if not first:
                            pe.wait_ge(free, n * NT + t - NT + 1)
                        out = acc[:, t, 0:width]
                        for k in range(KT):
                            xh, xl = hi[:, k, t * P:(t + 1) * P], lo[:, k, t * P:(t + 1) * P]
                            pe.matmul(out, xh, whi[b][:, k, 0:width], start=(k == 0), stop=False)
                            pe.matmul(out, xh, wlo[b][:, k, 0:width], start=False, stop=False)
                            mm = pe.matmul(out, xl, whi[b][:, k, 0:width], start=False, stop=(k == KT - 1))
                        mm.then_inc(s.acc_ready, 1)

                if to_dram is None:
                    for n in range(n_slots):
                        slot(n, n % 2, SLOT, first=(n == 0))
                    return
                slot(0, 0, SLOT, first=True)
                slot(1, 1, SLOT)
                with pe.Fori(1, full // 2) as i:
                    for b in range(2):
                        slot(2 * i + b, b, SLOT)
                if rest:
                    slot(full, 0, rest)




def mlp(nc, w1, w2, hi, lo, h):
    FF = 2 * P
    G = DFF // FF
    with ExitStack() as c:
        raw1 = c.enter_context(nc.sbuf_tensor("mlp_raw1", [P, KT, FF], F32))
        raw2 = c.enter_context(nc.sbuf_tensor("mlp_raw2", [P, 2, D], F32))
        w1hi = c.enter_context(nc.sbuf_tensor("mlp_w1hi", [P, KT, FF], F32R))
        w1lo = c.enter_context(nc.sbuf_tensor("mlp_w1lo", [P, KT, FF], F32R))
        w2hi = c.enter_context(nc.sbuf_tensor("mlp_w2hi", [P, 2, D], F32R))
        w2lo = c.enter_context(nc.sbuf_tensor("mlp_w2lo", [P, 2, D], F32R))
        ahi = [c.enter_context(nc.sbuf_tensor(f"mlp_ahi{i}", [P, 2, T], F32R)) for i in range(2)]
        alo = [c.enter_context(nc.sbuf_tensor(f"mlp_alo{i}", [P, 2, T], F32R)) for i in range(2)]
        relu = c.enter_context(nc.sbuf_tensor("mlp_relu", [P, 2, 512], F32))
        square = c.enter_context(nc.sbuf_tensor("mlp_square", [P, 2, 512], F32))
        hid = c.enter_context(nc.psum_tensor("mlp_hid", [P, 4, 512], F32))
        out = c.enter_context(nc.psum_tensor("mlp_out", [P, 4, 512], F32))
        s = c.enter_context(phase(nc, "w1_loaded", "w2_loaded", "w1hi_ready", "w1lo_ready", "w2hi_ready",
                                  "w2lo_ready", "hid_ready", "relu_ready", "square_ready", "ahi_ready",
                                  "alo_ready", "out_ready", "added", "scaled"))
        w1_v = w1.rearrange("(k p) f -> p k f", p=P)
        w2_v = w2.rearrange("(g j p) c -> g p j c", p=P, j=2)
        HB, OB = 4, 2 * NT

        with nc.Block() as block:
            @block.sync
            def _(sp):
                def load1(g):
                    sp.dma_start(raw1[:], w1_v[:, :, bass.ds(g * FF, FF)]).then_inc(s.w1_loaded, 16)

                def load2(g):
                    sp.dma_start(raw2[:], w2_v[g, :, :, :]).then_inc(s.w2_loaded, 16)

                load1(0)
                load2(0)
                with sp.Fori(1, G) as g:
                    sp.wait_ge(s.w1lo_ready, g)
                    load1(g)
                    sp.wait_ge(s.w2lo_ready, g)
                    load2(g)

            @block.scalar
            def _(act):
                def split1(g, first=False):
                    act.wait_ge(s.w1_loaded, 16 * g + 16)
                    if not first:
                        act.wait_ge(s.hid_ready, HB * g)
                    act.activation(w1hi[:], raw1[:], ACT.Copy).then_inc(s.w1hi_ready, 1)

                def split2(g, first=False):
                    act.wait_ge(s.w2_loaded, 16 * g + 16)
                    if not first:
                        act.wait_ge(s.out_ready, OB * g)
                    act.activation(w2hi[:], raw2[:], ACT.Copy).then_inc(s.w2hi_ready, 1)

                def hidden(g, buf, first=False):
                    for n in range(HB + 1):
                        if n < HB:
                            act.wait_ge(s.hid_ready, HB * g + n + 1)
                            if not first or n >= 2:
                                act.wait_ge(s.square_ready, HB * g + n - 1)
                            act.activation(relu[:, n % 2, :], hid[:, n, :], ACT.Relu).then_inc(s.relu_ready, 1)
                        if n:
                            j, half = (n - 1) // 2, (n - 1) % 2
                            act.wait_ge(s.square_ready, HB * g + n)
                            act.activation(ahi[buf][:, j, half * 512:(half + 1) * 512], square[:, (n - 1) % 2, :],
                                           ACT.Copy).then_inc(s.ahi_ready, 1)

                split1(0, first=True)
                hidden(0, 0, first=True)
                split1(1)
                split2(0, first=True)
                hidden(1, 1)
                split1(2)
                split2(1)
                hidden(2, 0)
                split1(3)
                with act.Fori(1, G // 2 - 1) as i:
                    for b in range(2):
                        g = 2 * i + b + 1
                        split2(g - 1)
                        hidden(g, (b + 1) % 2)
                        split1(g + 1)
                split2(G - 2)
                hidden(G - 1, 1)
                split2(G - 1)

            @block.vector
            def _(dve):
                def split1(g):
                    dve.wait_ge(s.w1hi_ready, g + 1)
                    dve.tensor_tensor(w1lo[:], raw1[:], w1hi[:].bitcast(F32), ALU.subtract).then_inc(s.w1lo_ready, 1)

                def split2(g):
                    dve.wait_ge(s.w2hi_ready, g + 1)
                    dve.tensor_tensor(w2lo[:], raw2[:], w2hi[:].bitcast(F32), ALU.subtract).then_inc(s.w2lo_ready, 1)

                def hidden(g, buf, first=False):
                    for n in range(HB + 1):
                        if n < HB:
                            dve.wait_ge(s.relu_ready, HB * g + n + 1)
                            if not first or n >= 2:
                                dve.wait_ge(s.ahi_ready, HB * g + n - 1)
                                dve.wait_ge(s.alo_ready, HB * g + n - 1)
                            dve.tensor_tensor(square[:, n % 2, :], relu[:, n % 2, :], relu[:, n % 2, :],
                                              ALU.mult).then_inc(s.square_ready, 1)
                        if n:
                            j, half = (n - 1) // 2, (n - 1) % 2
                            part = slice(half * 512, (half + 1) * 512)
                            dve.wait_ge(s.ahi_ready, HB * g + n)
                            dve.tensor_tensor(alo[buf][:, j, part], square[:, (n - 1) % 2, :],
                                              ahi[buf][:, j, part].bitcast(F32), ALU.subtract).then_inc(s.alo_ready, 1)

                def add_out(g, first=False):
                    if not first:
                        dve.wait_ge(s.added, OB * g)
                    for m in range(OB):
                        t, half = m // 2, m % 2
                        part = h[:, t, half * 512:(half + 1) * 512]
                        dve.wait_ge(s.out_ready, OB * g + m + 1)
                        dve.tensor_tensor(part, part, out[:, m % 4, :], ALU.add).then_inc(s.added, 1)

                split1(0)
                dve.tensor_scalar(h[:], h[:], ALPHA, None, ALU.mult).then_inc(s.scaled, 1)
                hidden(0, 0, first=True)
                split1(1)
                dve.wait_ge(s.scaled, 1)
                split2(0)
                hidden(1, 1)
                split1(2)
                add_out(0, first=True)
                split2(1)
                hidden(2, 0)
                split1(3)
                add_out(1)
                with dve.Fori(1, G // 2 - 1) as i:
                    for b in range(2):
                        g = 2 * i + b + 1
                        split2(g - 1)
                        hidden(g, (b + 1) % 2)
                        split1(g + 1)
                        add_out(g - 1)
                split2(G - 2)
                hidden(G - 1, 1)
                add_out(G - 2)
                split2(G - 1)
                add_out(G - 1)

            @block.tensor
            def _(pe):
                def up(g, first=False):
                    pe.wait_ge(s.w1lo_ready, g + 1)
                    for n in range(HB):
                        j, half = n // 2, n % 2
                        if not first:
                            pe.wait_ge(s.relu_ready, HB * (g - 1) + n + 1)
                        for k in range(KT):
                            wh, wl = w1hi[:, k, j * P:(j + 1) * P], w1lo[:, k, j * P:(j + 1) * P]
                            xh, xl = hi[:, k, half * 512:(half + 1) * 512], lo[:, k, half * 512:(half + 1) * 512]
                            pe.matmul(hid[:, n, :], wh, xh, start=(k == 0), stop=False)
                            pe.matmul(hid[:, n, :], wh, xl, start=False, stop=False)
                            mm = pe.matmul(hid[:, n, :], wl, xh, start=False, stop=(k == KT - 1))
                        mm.then_inc(s.hid_ready, 1)

                def down(g, buf, first=False):
                    pe.wait_ge(s.w2lo_ready, g + 1)
                    pe.wait_ge(s.alo_ready, HB * g + HB)
                    for m in range(OB):
                        t, half = m // 2, m % 2
                        if not first or m >= 4:
                            pe.wait_ge(s.added, OB * g + m - 3)
                        for j in range(2):
                            xh, xl = ahi[buf][:, j, t * P:(t + 1) * P], alo[buf][:, j, t * P:(t + 1) * P]
                            wh, wl = w2hi[:, j, half * 512:(half + 1) * 512], w2lo[:, j, half * 512:(half + 1) * 512]
                            pe.matmul(out[:, m % 4, :], xh, wh, start=(j == 0), stop=False)
                            pe.matmul(out[:, m % 4, :], xh, wl, start=False, stop=False)
                            mm = pe.matmul(out[:, m % 4, :], xl, wh, start=False, stop=(j == 1))
                        mm.then_inc(s.out_ready, 1)

                up(0, first=True)
                up(1)
                down(0, 0, first=True)
                up(2)
                down(1, 1)
                with pe.Fori(1, G // 2 - 1) as i:
                    for b in range(2):
                        g = 2 * i + b + 1
                        up(g)
                        down(g - 1, b)
                up(G - 1)
                down(G - 2, 0)
                down(G - 1, 1)


def retention(nc, tag, proj, tab, ident, y):
    with ExitStack() as c:
        sb = lambda n, shape: c.enter_context(nc.sbuf_tensor(f"{tag}_{n}", shape, F32))
        ps = lambda n, shape: c.enter_context(nc.psum_tensor(f"{tag}_{n}", shape, F32))
        qkvg = sb("qkvg", [P, NT, 4 * GW])
        rope, decay = sb("rope", [P, NT, HD]), sb("decay", [P, H, P])
        zeta, xi, chunk = sb("zeta", [P, H]), sb("xi", [P, H]), sb("chunk", [P, H])
        qk = sb("qk", [P, NT, 2 * H, HD])
        t1, t2 = sb("t1", [P, NT, 2 * H, HD // 2]), sb("t2", [P, NT, 2 * H, HD // 2])
        t3, t4 = sb("t3", [P, NT, 2 * H, HD // 2]), sb("t4", [P, NT, 2 * H, HD // 2])
        zv = sb("zv", [P, NT, H, HD])
        qT, kT = sb("qT", [HD, H, P]), sb("kT", [HD, H, P])
        sc, cross = sb("sc", [P, H, P]), sb("cross", [P, H, HD])
        state = sb("state", [HD, H, HD])
        sq, ss, rr = sb("sq", [P, NT * H, HD]), sb("ss", [P, NT * H]), sb("rr", [P, NT * H])
        sg, power = sb("sg", [P, NT, GW]), sb("power", [P, NT * H])
        psq, psk = ps("psq", [HD, H, P]), ps("psk", [HD, H, P])
        pss, psy = ps("pss", [P, H, P]), ps("psy", [P, 512])
        psx, pskv = ps("psx", [P, 512]), ps("pskv", [HD, 512])
        s = c.enter_context(phase(nc, "loaded", "tables", "products", "rotated", "zv_ready", "turned", "q_copied",
                                  "k_copied", "scored", "decayed", "y_ready", "crossed", "y_out", "kv_ready",
                                  "state_decayed", "state_ready", "squared", "summed", "meaned", "rooted",
                                  "tanh_ready", "gated", "gate_mul", "normed", "power_set"))
        yv = y.rearrange("p t (h d) -> p t h d", d=HD)
        q_in = qkvg[:, :, 0:2 * GW].rearrange("p t (h d) -> p t h d", d=HD)
        x1, x2 = q_in[:, :, :, 0:HD // 2], q_in[:, :, :, HD // 2:HD]
        cos = rope[:, :, 0:HD // 2].unsqueeze(2).to_broadcast([P, NT, 2 * H, HD // 2])
        sin = rope[:, :, HD // 2:HD].unsqueeze(2).to_broadcast([P, NT, 2 * H, HD // 2])
        v = qkvg[:, :, 2 * GW:3 * GW].rearrange("p t (h d) -> p t h d", d=HD)
        g = qkvg[:, :, 3 * GW:4 * GW]

        with nc.Block() as block:
            @block.sync
            def _(sp):
                sp.dma_start(qkvg[:], tokens(proj, COL["rq"], COL["rq"] + 4 * GW)).then_inc(s.loaded, 16)
                sp.dma_start(rope[:], tab["t_rope_ret"]).then_inc(s.tables, 16)
                sp.dma_start(decay[:], tab["t_decay"]).then_inc(s.tables, 16)
                sp.dma_start(zeta[:], tab["t_zeta"]).then_inc(s.tables, 16)
                sp.dma_start(xi[:], tab["t_xi"]).then_inc(s.tables, 16)
                sp.dma_start(chunk[:], tab["t_chunk"]).then_inc(s.tables, 16)

            @block.gpsimd
            def _(pool):
                pool.memset(power[:], -0.5).then_inc(s.power_set, 1)
                pool.wait_ge(s.loaded, 16)
                pool.wait_ge(s.tables, 80)
                pool.tensor_tensor(t3[:], x1, sin, ALU.mult).then_inc(s.products, 1)
                pool.tensor_tensor(t4[:], x2, cos, ALU.mult).then_inc(s.products, 1)
                pool.wait_ge(s.power_set, 1)
                pool.wait_ge(s.meaned, 1)
                pool.tensor_tensor(rr[:], ss[:], power[:], ALU.pow).then_inc(s.rooted, 1)

            @block.vector
            def _(dve):
                dve.wait_ge(s.loaded, 16)
                dve.wait_ge(s.tables, 80)
                dve.tensor_tensor(t1[:], x1, cos, ALU.mult)
                dve.tensor_tensor(t2[:], x2, sin, ALU.mult).then_inc(s.products, 1)
                dve.tensor_tensor(zv[:], v, zeta[:].unsqueeze(1).unsqueeze(3).to_broadcast([P, NT, H, HD]),
                                  ALU.mult).then_inc(s.zv_ready, 1)
                dve.wait_ge(s.products, 3)
                dve.tensor_tensor(qk[:, :, :, 0:HD // 2], t1[:], t2[:], ALU.subtract).then_inc(s.rotated, 1)
                dve.tensor_tensor(qk[:, :, :, HD // 2:HD], t3[:], t4[:], ALU.add).then_inc(s.rotated, 1)
                for t in range(NT):
                    dve.wait_ge(s.turned, t + 1)
                    if t:
                        dve.wait_ge(s.scored, t)
                        dve.wait_ge(s.y_ready, t)
                    dve.tensor_copy(kT[:], psk[:]).then_inc(s.k_copied, 1)
                    dve.wait_ge(s.scored, t + 1)
                    dve.tensor_tensor(sc[:], pss[:], decay[:], ALU.mult).then_inc(s.decayed, 1)
                    dve.wait_ge(s.y_ready, t + 1)
                    if t:
                        xib = xi[:].unsqueeze(2).to_broadcast([P, H, HD])
                        dve.tensor_tensor(cross[:], psx[:, 0:GW].rearrange("p (h d) -> p h d", d=HD), xib,
                                          ALU.mult).then_inc(s.crossed, 1)
                        dve.wait_ge(s.crossed, t)
                        dve.tensor_tensor(yv[:, t, :, :], cross[:], psy[:, 0:GW].rearrange("p (h d) -> p h d", d=HD),
                                          ALU.add).then_inc(s.y_out, 1)
                        if t < NT - 1:
                            dve.wait_ge(s.state_ready, t)
                            dve.tensor_tensor(state[:], state[:], chunk[0:HD, :].unsqueeze(2).to_broadcast([HD, H, HD]),
                                              ALU.mult).then_inc(s.state_decayed, 1)
                            dve.wait_ge(s.state_decayed, t)
                            dve.wait_ge(s.kv_ready, t + 1)
                            dve.tensor_tensor(state[:], state[:], pskv[:, 0:GW].rearrange("p (h d) -> p h d", d=HD),
                                              ALU.add).then_inc(s.state_ready, 1)
                    else:
                        dve.tensor_copy(yv[:, t, :, :], psy[:, 0:GW].rearrange("p (h d) -> p h d", d=HD)).then_inc(s.y_out, 1)
                        dve.wait_ge(s.kv_ready, 1)
                        dve.tensor_copy(state[:], pskv[:, 0:GW].rearrange("p (h d) -> p h d", d=HD)).then_inc(s.state_ready, 1)
                dve.wait_ge(s.squared, 1)
                dve.tensor_reduce(ss[:], sq[:], AX.X, ALU.add).then_inc(s.summed, 1)
                dve.wait_ge(s.tanh_ready, 1)
                dve.tensor_scalar(sg[:], sg[:], 0.5, 0.5, ALU.mult, ALU.add).then_inc(s.gated, 1)
                dve.wait_ge(s.summed, 1)
                dve.tensor_scalar(ss[:], ss[:], 1.0 / HD, EPS, ALU.mult, ALU.add).then_inc(s.meaned, 1)
                dve.wait_ge(s.gated, 1)
                dve.tensor_tensor(sg[:], sg[:], g, ALU.mult).then_inc(s.gate_mul, 1)
                dve.wait_ge(s.rooted, 1)
                dve.wait_ge(s.y_out, NT)
                yh = y.rearrange("p t (h d) -> p t h d", d=HD)
                dve.tensor_tensor(yh, yh, rr[:].rearrange("p (t h) -> p t h", h=H).unsqueeze(3).to_broadcast([P, NT, H, HD]),
                                  ALU.mult).then_inc(s.normed, 1)
                dve.wait_ge(s.normed, 1)
                dve.wait_ge(s.gate_mul, 1)
                dve.tensor_tensor(y, y, sg[:], ALU.mult)

            @block.scalar
            def _(act):
                act.wait_ge(s.loaded, 16)
                act.activation(sg[:], g, ACT.Tanh, scale=0.5).then_inc(s.tanh_ready, 1)
                for t in range(NT):
                    act.wait_ge(s.turned, t + 1)
                    if t:
                        act.wait_ge(s.y_ready, t)
                    act.activation(qT[:], psq[:], ACT.Copy).then_inc(s.q_copied, 1)
                act.wait_ge(s.y_out, NT)
                act.activation(sq[:].rearrange("p (t h) d -> p t h d", h=H), yv, ACT.Square).then_inc(s.squared, 1)

            @block.tensor
            def _(pe):
                def turn(t):
                    if t:
                        pe.wait_ge(s.q_copied, t)
                        pe.wait_ge(s.k_copied, t)
                    for h in range(H):
                        pe.transpose(psq[:, h, :], qk[:, t, h, :], ident[:])
                        mm = pe.transpose(psk[:, h, :], qk[:, t, H + h, :], ident[:])
                    mm.then_inc(s.turned, 1)

                pe.wait_ge(s.rotated, 2)
                turn(0)
                for t in range(NT):
                    pe.wait_ge(s.q_copied, t + 1)
                    pe.wait_ge(s.k_copied, t + 1)
                    if t:
                        pe.wait_ge(s.decayed, t)
                    for h in range(H):
                        mm = pe.matmul(pss[:, h, :], kT[:, h, :], qT[:, h, :], start=True, stop=True)
                    mm.then_inc(s.scored, 1)
                    if t < NT - 1:
                        turn(t + 1)
                    pe.wait_ge(s.zv_ready, 1)
                    if t:
                        pe.wait_ge(s.state_ready, t)
                    if t < NT - 1:
                        for h in range(H):
                            mm = pe.matmul(pskv[:, h * HD:(h + 1) * HD], qk[:, t, H + h, :], zv[:, t, h, :],
                                           start=True, stop=True)
                        mm.then_inc(s.kv_ready, 1)
                    if t:
                        pe.wait_ge(s.y_out, t)
                        for h in range(H):
                            pe.matmul(psx[:, h * HD:(h + 1) * HD], qT[:, h, :], state[:, h, :], start=True, stop=True)
                    pe.wait_ge(s.decayed, t + 1)
                    for h in range(H):
                        mm = pe.matmul(psy[:, h * HD:(h + 1) * HD], sc[:, h, :], v[:, t, h, :], start=True, stop=True)
                    mm.then_inc(s.y_ready, 1)


def ssd(nc, tag, proj, tab, w, ident, y):
    NC = XBC // P
    with ExitStack() as c:
        sb = lambda n, shape: c.enter_context(nc.sbuf_tensor(f"{tag}_{n}", shape, F32))
        ps = lambda n, shape: c.enter_context(nc.psum_tensor(f"{tag}_{n}", shape, F32))
        z, xbc, dtr = sb("z", [P, NT, GW]), sb("xbc", [P, NT, XBC]), sb("dtr", [P, NT, H])
        upto, later, ones = sb("upto", [P, P]), sb("later", [P, P]), sb("ones", [P, P])
        cw, cb = sb("cw", [P, NC, CONV]), sb("cb", [P, NC])
        dtb, alog, skip, gain = sb("dtb", [P, H]), sb("alog", [P, H]), sb("skip", [P, H]), sb("gain", [P, GW])
        xT = sb("xT", [P, NC, T + CONV - 1])
        th = sb("th", [P, T])
        xc = sb("xc", [P, NC, T])
        xb = sb("xb", [P, NT, 2 * GW])
        u, v1, v2, v3, v4 = (sb(n, [P, NT, H]) for n in ("u", "v1", "v2", "v3", "v4"))
        dt, a, acs, eacs, tot, etot, dend = (sb(n, [P, NT, H]) for n in ("dt", "a", "acs", "eacs", "tot", "etot", "dend"))
        nega = sb("nega", [P, H])
        xdt, xdd = sb("xdt", [P, NT, H, HD]), sb("xdd", [P, NT, H, HD])
        E, m = sb("E", [P, H, P]), sb("m", [P, H, P])
        off = sb("off", [P, H, HD])
        state = sb("state", [STATE, H, HD])
        ss, rr, power = sb("ss", [P, NT]), sb("rr", [P, NT]), sb("power", [P, NT])
        bank = [ps(f"bank{i}", [P, 512]) for i in range(8)]
        s = c.enter_context(phase(nc, "xbc_loaded", "loaded", "consts", "halved", "x_turned", "x_copied", "conv_step", "conv_done",
                                  "tanh_done", "silu_done", "b_turned", "b_copied", "dt_step", "dt_exp", "dt_ready",
                                  "a_exp", "a_neg", "a_ready", "sums_ready", "sums_copied", "exps_ready", "dend_ready",
                                  "xdt_ready", "xdd_ready", "rows_ready", "cb_ready", "e_step", "e_ready", "m_ready",
                                  "diag_ready", "y_step", "y_out", "new_ready", "state_step", "state_ready",
                                  "z_tanh", "gate_step", "squared", "meaned", "rooted", "power_set"))
        yv = y.rearrange("p t (h d) -> p t h d", d=HD)
        xh = xb[:, :, 0:GW].rearrange("p t (h d) -> p t h d", d=HD)
        per = lambda ap: ap.unsqueeze(3).to_broadcast([P, NT, H, HD])
        heads = lambda ap: ap[:, 0:GW].rearrange("p (h d) -> p h d", d=HD)
        bc = lambda ap: ap.unsqueeze(1).to_broadcast([P, NT, H])

        with nc.Block() as block:
            @block.sync
            def _(sp):
                sp.dma_start(xbc[:], tokens(proj, COL["xbc"], COL["xbc"] + XBC)).then_inc(s.xbc_loaded, 16)
                with nc.allow_non_contiguous_dma(reason="a few KB of conv weights, turned"):
                    for k in range(CONV):
                        sp.dma_start(cw[:, :, k], w["conv_w"][k].rearrange("(c p) -> p c", p=P)).then_inc(s.consts, 16)
                    sp.dma_start(cb[:], w["conv_b"].rearrange("(c p) -> p c", p=P)).then_inc(s.consts, 16)
                sp.dma_start(dtr[:], tokens(proj, COL["dt"], COL["dt"] + H)).then_inc(s.loaded, 16)
                sp.dma_start(dtb[:], w["dt_bias"].partition_broadcast(P)).then_inc(s.loaded, 16)
                sp.dma_start(alog[:], w["a_log"].partition_broadcast(P)).then_inc(s.loaded, 16)
                sp.dma_start(skip[:], w["d_skip"].partition_broadcast(P)).then_inc(s.loaded, 16)
                sp.dma_start(gain[:], w["ssm_norm_g"].partition_broadcast(P)).then_inc(s.loaded, 16)
                sp.dma_start(upto[:], tab["t_upto"]).then_inc(s.loaded, 16)
                sp.dma_start(later[:], tab["t_later"]).then_inc(s.loaded, 16)
                sp.dma_start(z[:], tokens(proj, COL["z"], COL["z"] + GW)).then_inc(s.loaded, 16)

            @block.gpsimd
            def _(pool):
                pool.memset(ones[:], 1.0).then_inc(s.power_set, 1)
                pool.memset(xT[:, :, 0:CONV - 1], 0.0).then_inc(s.power_set, 1)
                pool.memset(power[:], -0.5).then_inc(s.power_set, 1)
                pool.wait_ge(s.b_copied, NT)
                pool.wait_ge(s.dt_ready, 1)
                pool.tensor_tensor(xdt[:], xh, per(dt[:]), ALU.mult).then_inc(s.xdt_ready, 1)
                pool.wait_ge(s.dend_ready, 1)
                pool.wait_ge(s.xdt_ready, 1)
                pool.tensor_tensor(xdd[:], xdt[:], per(dend[:]), ALU.mult).then_inc(s.xdd_ready, 1)
                pool.tensor_tensor(yv, xh, skip[:].unsqueeze(1).unsqueeze(3).to_broadcast([P, NT, H, HD]),
                                   ALU.mult).then_inc(s.xdd_ready, 1)
                pool.wait_ge(s.meaned, 1)
                pool.wait_ge(s.power_set, 3)
                pool.tensor_tensor(rr[:], ss[:], power[:], ALU.pow).then_inc(s.rooted, 1)

            @block.tensor
            def _(pe):
                pe.wait_ge(s.xbc_loaded, 16)
                for n in range(2 * NC):
                    ch, half = n // 2, n % 2
                    if n >= 4:
                        pe.wait_ge(s.x_copied, n - 3)
                    for j in range(4):
                        mm = pe.transpose(bank[4 + n % 4][:, j * P:(j + 1) * P], xbc[:, 4 * half + j, ch * P:(ch + 1) * P], ident[:])
                    mm.then_inc(s.x_turned, 1)
                pe.wait_ge(s.a_ready, 1)
                pe.wait_ge(s.x_copied, 2 * NC)
                pe.wait_ge(s.power_set, 1)
                af = a[:].rearrange("p t h -> p (t h)")
                pe.matmul(bank[4][:, 0:NT * H], upto[:], af, start=True, stop=True)
                pe.matmul(bank[4][:, NT * H:2 * NT * H], ones[:], af, start=True, stop=True,
                          skip_group_check=True).then_inc(s.sums_ready, 1)
                pe.wait_ge(s.silu_done, 4)
                pe.wait_ge(s.sums_copied, 1)
                for t in range(NT):
                    if t >= 2:
                        pe.wait_ge(s.b_copied, t - 1)
                    for j in range(4):
                        mm = pe.transpose(bank[6 + t % 2][:, j * P:(j + 1) * P], xc[:, j, t * P:(t + 1) * P], ident[:])
                    mm.then_inc(s.b_turned, 1)

                def rows(t):
                    if t:
                        pe.wait_ge(s.e_step, 2 * t)
                    else:
                        pe.wait_ge(s.silu_done, NC)
                        pe.wait_ge(s.b_copied, NT)
                    for h in range(H):
                        mm = pe.matmul(bank[0][:, h * P:(h + 1) * P], a[:, t, h:h + 1].to_broadcast([P, P]), upto[:],
                                       start=True, stop=True)
                    mm.then_inc(s.rows_ready, 1)

                rows(0)
                for t in range(NT):
                    here = slice(t * P, (t + 1) * P)
                    if t:
                        pe.wait_ge(s.m_ready, t)
                    for g in range(2):
                        mm = pe.matmul(bank[1][:, g * P:(g + 1) * P], xc[:, 2 + g, here], xc[:, 4 + g, here],
                                       start=True, stop=True)
                    mm.then_inc(s.cb_ready, 1)
                    if t < NT - 1:
                        rows(t + 1)
                        pe.wait_ge(s.xdd_ready, 1)
                        if t:
                            pe.wait_ge(s.state_ready, t)
                        for g in range(2):
                            mm = pe.matmul(bank[4][:, g * P:(g + 1) * P], xb[:, t, GW + g * P:GW + (g + 1) * P],
                                           xdd[:, t, 2 * g:2 * g + 2, :], start=True, stop=True)
                        mm.then_inc(s.new_ready, 1)
                    if t:
                        pe.wait_ge(s.state_ready, t)
                        pe.wait_ge(s.y_out, t)
                        for g in range(2):
                            pe.matmul(bank[3][:, g * P:(g + 1) * P], xc[:, 4 + g, here], state[:, 2 * g:2 * g + 2, :],
                                      start=True, stop=True)
                    pe.wait_ge(s.m_ready, t + 1)
                    for h in range(H):
                        mm = pe.matmul(bank[2][:, h * HD:(h + 1) * HD], m[:, h, :], xdt[:, t, h, :], start=True, stop=True)
                    mm.then_inc(s.diag_ready, 1)

            @block.scalar
            def _(act):
                for n in range(2 * NC):
                    ch, half = n // 2, n % 2
                    act.wait_ge(s.x_turned, n + 1)
                    act.activation(xT[:, ch, CONV - 1 + half * 512:CONV - 1 + (half + 1) * 512], bank[4 + n % 4][:],
                                   ACT.Copy).then_inc(s.x_copied, 1)
                act.wait_ge(s.loaded, 128)
                act.activation(nega[:], alog[:], ACT.Exp).then_inc(s.a_exp, 1)
                act.wait_ge(s.dt_step, 2)
                act.activation(u[:], v2[:], ACT.Exp).then_inc(s.dt_exp, 1)
                for ch in range(NC):
                    act.wait_ge(s.conv_done, ch + 1)
                    if ch:
                        act.wait_ge(s.silu_done, ch)
                    b = 2 * (ch % 2)
                    for half in range(2):
                        i = act.activation(th[:, half * 512:(half + 1) * 512], bank[b + half][:], ACT.Tanh)
                    i.then_inc(s.tanh_done, 1)
                    if ch == 1:
                        act.wait_ge(s.sums_copied, 1)
                        act.activation(eacs[:], acs[:], ACT.Exp)
                        act.activation(etot[:], tot[:], ACT.Exp).then_inc(s.exps_ready, 1)
                        act.activation(dend[:], v4[:], ACT.Exp).then_inc(s.dend_ready, 1)
                for t in range(NT):
                    act.wait_ge(s.b_turned, t + 1)
                    act.activation(xb[:, t, :], bank[6 + t % 2][:], ACT.Copy).then_inc(s.b_copied, 1)
                for t in range(NT):
                    act.wait_ge(s.e_step, 2 * t + 2)
                    act.activation(E[:], E[:], ACT.Exp).then_inc(s.e_ready, 1)
                act.activation(th[:].rearrange("p (a b) -> p a b", a=4), z[:, 0:4, :], ACT.Tanh, scale=0.5).then_inc(s.z_tanh, 1)
                act.wait_ge(s.gate_step, 1)
                act.activation(th[:].rearrange("p (a b) -> p a b", a=4), z[:, 4:8, :], ACT.Tanh, scale=0.5).then_inc(s.z_tanh, 1)
                act.wait_ge(s.gate_step, 4)
                for t in range(NT):
                    i = act.activation(xbc[:, t, 0:GW], y[:, t, :], ACT.Square, accum_out=ss[:, t:t + 1])
                i.then_inc(s.squared, 1)

            @block.vector
            def _(dve):
                dve.wait_ge(s.loaded, 128)
                n = [0]

                def step(i):
                    n[0] += 1
                    i.then_inc(s.dt_step, 1)
                    dve.wait_ge(s.dt_step, n[0])

                step(dve.tensor_tensor(v1[:], dtr[:], bc(dtb[:]), ALU.add))
                step(dve.scalar_tensor_tensor(v2[:], v1[:], -1.0, v1[:], ALU.mult, ALU.min))
                step(dve.tensor_scalar(v1[:], v1[:], 0.0, None, ALU.max))
                dve.wait_ge(s.dt_exp, 1)
                step(dve.tensor_scalar(v2[:], u[:], 2.0, None, ALU.add))
                step(dve.reciprocal(v3[:], v2[:]))
                step(dve.tensor_tensor(u[:], u[:], v3[:], ALU.mult))
                step(dve.tensor_tensor(v2[:], u[:], u[:], ALU.mult))
                step(dve.tensor_scalar(v3[:], v2[:], 1.0 / 17, None, ALU.mult))
                for k in range(7, 0, -1):
                    step(dve.scalar_tensor_tensor(v3[:], v3[:], 1.0 / (2 * k + 1), v2[:], ALU.add, ALU.mult))
                step(dve.scalar_tensor_tensor(v3[:], v3[:], 1.0, u[:], ALU.add, ALU.mult))
                step(dve.scalar_tensor_tensor(dt[:], v3[:], 2.0, v1[:], ALU.mult, ALU.add))
                dve.wait_ge(s.a_exp, 1)
                dve.scalar_tensor_tensor(a[:], dt[:], -1.0, bc(nega[:]), ALU.mult, ALU.mult).then_inc(s.a_ready, 1)
                dve.sem_inc(s.dt_ready, 1)
                dve.wait_ge(s.consts, 80)
                dve.tensor_scalar(cw[:], cw[:], 0.5, None, ALU.mult).then_inc(s.halved, 1)
                dve.tensor_scalar(cb[:], cb[:], 0.5, None, ALU.mult).then_inc(s.halved, 1)
                dve.wait_ge(s.halved, 2)
                dve.wait_ge(s.power_set, 2)
                st = 0
                for ch in range(NC):
                    dve.wait_ge(s.x_copied, 2 * ch + 2)
                    b = 2 * (ch % 2)
                    for k in range(CONV):
                        if k:
                            dve.wait_ge(s.conv_step, st)
                        for half in range(2):
                            src = xT[:, ch, k + half * 512:k + half * 512 + 512]
                            acc = bank[b + half][:]
                            if k == 0:
                                i = dve.tensor_scalar(acc, src, cw[:, ch, 0:1], cb[:, ch:ch + 1], ALU.mult, ALU.add)
                            else:
                                i = dve.scalar_tensor_tensor(acc, src, cw[:, ch, k:k + 1], acc, ALU.mult, ALU.add)
                        if k < CONV - 1:
                            st += 1
                            i.then_inc(s.conv_step, 1)
                    i.then_inc(s.conv_done, 1)
                    dve.wait_ge(s.tanh_done, ch + 1)
                    dve.wait_ge(s.conv_done, ch + 1)
                    for half in range(2):
                        i = dve.scalar_tensor_tensor(xc[:, ch, half * 512:(half + 1) * 512], th[:, half * 512:(half + 1) * 512], 1.0,
                                                     bank[b + half][:], ALU.add, ALU.mult)
                    i.then_inc(s.silu_done, 1)
                    if ch == 0:
                        dve.wait_ge(s.sums_ready, 1)
                        dve.tensor_copy(acs[:], bank[4][:, 0:NT * H].rearrange("p (t h) -> p t h", h=H)).then_inc(s.state_step, 1)
                        dve.tensor_copy(tot[:], bank[4][:, NT * H:2 * NT * H].rearrange("p (t h) -> p t h", h=H)).then_inc(s.state_step, 1)
                        dve.wait_ge(s.state_step, 2)
                        dve.tensor_tensor(v4[:], tot[:], acs[:], ALU.subtract).then_inc(s.sums_copied, 1)

                def expo(t):
                    dve.wait_ge(s.rows_ready, t + 1)
                    if t:
                        dve.wait_ge(s.m_ready, t)
                    dve.tensor_tensor(E[:], bank[0][:].rearrange("p (h l) -> p h l", h=H),
                                      acs[:, t, :].unsqueeze(2).to_broadcast([P, H, P]), ALU.subtract).then_inc(s.e_step, 1)
                    dve.wait_ge(s.e_step, 2 * t + 1)
                    dve.tensor_tensor(E[:], E[:], later[:].unsqueeze(1).to_broadcast([P, H, P]), ALU.add).then_inc(s.e_step, 1)

                expo(0)
                for t in range(NT):
                    dve.wait_ge(s.e_ready, t + 1)
                    dve.wait_ge(s.cb_ready, t + 1)
                    if t:
                        dve.wait_ge(s.diag_ready, t)
                    dve.tensor_tensor(m[:].rearrange("p (g r) l -> p g r l", g=2), E[:].rearrange("p (g r) l -> p g r l", g=2),
                                      bank[1][:, 0:2 * P].rearrange("p (g l) -> p g l", g=2).unsqueeze(2).to_broadcast([P, 2, 2, P]),
                                      ALU.mult).then_inc(s.m_ready, 1)
                    if t < NT - 1:
                        expo(t + 1)
                    dve.wait_ge(s.diag_ready, t + 1)
                    dve.wait_ge(s.xdd_ready, 2)
                    if t:
                        dve.wait_ge(s.exps_ready, 1)
                        dve.tensor_tensor(off[:], heads(bank[3]), eacs[:, t, :].unsqueeze(2).to_broadcast([P, H, HD]),
                                          ALU.mult).then_inc(s.y_step, 1)
                        dve.wait_ge(s.y_step, 2 * t - 1)
                        dve.tensor_tensor(off[:], off[:], heads(bank[2]), ALU.add).then_inc(s.y_step, 1)
                        dve.wait_ge(s.y_step, 2 * t)
                        dve.tensor_tensor(yv[:, t, :, :], yv[:, t, :, :], off[:], ALU.add).then_inc(s.y_out, 1)
                    else:
                        dve.tensor_tensor(yv[:, t, :, :], yv[:, t, :, :], heads(bank[2]), ALU.add).then_inc(s.y_out, 1)
                    if t < NT - 1:
                        dve.wait_ge(s.new_ready, t + 1)
                        if t:
                            dve.wait_ge(s.state_ready, t)
                            dve.tensor_tensor(state[:], state[:], etot[:, t, :].unsqueeze(2).to_broadcast([P, H, HD]),
                                              ALU.mult).then_inc(s.state_step, 1)
                            dve.wait_ge(s.state_step, t + 2)
                            dve.tensor_tensor(state[:], state[:], heads(bank[4]), ALU.add).then_inc(s.state_ready, 1)
                        else:
                            dve.tensor_copy(state[:], heads(bank[4])).then_inc(s.state_ready, 1)
                dve.wait_ge(s.y_out, NT)
                for i in range(2):
                    dve.wait_ge(s.z_tanh, i + 1)
                    zi, yi = z[:, 4 * i:4 * i + 4, :], y[:, 4 * i:4 * i + 4, :]
                    dve.scalar_tensor_tensor(zi, th[:].rearrange("p (a b) -> p a b", a=4), 1.0, zi, ALU.add,
                                             ALU.mult).then_inc(s.gate_step, 1)
                    dve.wait_ge(s.gate_step, 2 * i + 1)
                    dve.scalar_tensor_tensor(yi, zi, 0.5, yi, ALU.mult, ALU.mult).then_inc(s.gate_step, 1)
                dve.wait_ge(s.squared, 1)
                dve.tensor_scalar(ss[:], ss[:], 1.0 / GW, EPS, ALU.mult, ALU.add).then_inc(s.meaned, 1)
                dve.wait_ge(s.rooted, 1)
                for t in range(NT):
                    dve.scalar_tensor_tensor(y[:, t, :], y[:, t, :], rr[:, t:t + 1], gain[:], ALU.mult, ALU.mult)


def latent(nc, tag, proj, tab, w, ident, y):
    with ExitStack() as c:
        sb = lambda n, shape: c.enter_context(nc.sbuf_tensor(f"{tag}_{n}", shape, F32))
        qT, kT = sb("qT", [QD, H, T]), sb("kT", [QD, H, T])
        v, mask = sb("v", [P, NT, H, HD]), sb("mask", [P, T])
        with ExitStack() as c1:
            sb1 = lambda n, shape: c1.enter_context(nc.sbuf_tensor(f"{tag}_{n}", shape, F32))
            ps1 = lambda n, shape: c1.enter_context(nc.psum_tensor(f"{tag}_{n}", shape, F32))
            lat = sb1("lat", [P, NT, QR + KVR + ROPE])
            rope = sb1("rope", [P, NT, ROPE])
            wq, wkv = sb1("wq", [P, 2, H * QD]), sb1("wkv", [P, H * (NOPE + HD)])
            gq, gkv = sb1("gq", [P, 2]), sb1("gkv", [P, 1])
            junk, ss, rr, power = sb1("junk", [P, NT, QR + KVR]), sb1("ss", [P, 2, NT]), sb1("rr", [P, 2, NT]), sb1("power", [P, 2, NT])
            cT = sb1("cT", [P, 2, 3, P])
            qt, kt = sb1("qt", [P, NT, H, QD]), sb1("kt", [P, NT, H, QD])
            HR = ROPE // 2
            t1, t2, t3, t4 = (sb1(f"t{i}", [P, NT, H + 1, HR]) for i in range(4))
            pc, pq, pkv = ps1("pc", [P, 2, 512]), ps1("pq", [P, 512]), ps1("pkv", [P, 512])
            pT = ps1("pT", [P, 4, H, P])
            s = c1.enter_context(phase(nc, "lat_loaded", "loaded", "squared", "meaned", "rooted", "power_set", "weighted",
                                       "normed", "c_turned", "c_copied", "up_ready", "q_out", "k_out", "v_out",
                                       "products", "rotated", "qk_turned", "q_copied", "k_copied"))
            x = lambda ap, r: ap[:, :, :, r]
            with nc.Block() as block:
                @block.sync
                def _(sp):
                    sp.dma_start(lat[:], tokens(proj, COL["cq"], COL["rq"])).then_inc(s.lat_loaded, 16)
                    sp.dma_start(wq[:], w["w_uq"].rearrange("(k p) n -> p k n", p=P)).then_inc(s.loaded, 16)
                    sp.dma_start(wkv[:], w["w_ukv"]).then_inc(s.loaded, 16)
                    with nc.allow_non_contiguous_dma(reason="384 gains, one per partition"):
                        sp.dma_start(gq[:], w["q_norm_g"].rearrange("(k p) -> p k", p=P)).then_inc(s.loaded, 16)
                        sp.dma_start(gkv[:], w["kv_norm_g"].rearrange("(k p) -> p k", p=P)).then_inc(s.loaded, 16)
                    sp.dma_start(rope[:], tab["t_rope_mla"]).then_inc(s.loaded, 16)
                    sp.dma_start(mask[:], tab["t_causal"]).then_inc(s.loaded, 16)

                @block.gpsimd
                def _(pool):
                    pool.memset(power[:], -0.5).then_inc(s.power_set, 1)
                    pool.wait_ge(s.power_set, 1)
                    pool.wait_ge(s.meaned, 2)
                    pool.tensor_tensor(rr[:], ss[:], power[:], ALU.pow).then_inc(s.rooted, 1)

                @block.scalar
                def _(act):
                    act.wait_ge(s.lat_loaded, 16)
                    for t in range(NT):
                        act.activation(junk[:, t, 0:QR], lat[:, t, 0:QR], ACT.Square, accum_out=ss[:, 0, t:t + 1])
                        i = act.activation(junk[:, t, QR:QR + KVR], lat[:, t, QR:QR + KVR], ACT.Square, accum_out=ss[:, 1, t:t + 1])
                    i.then_inc(s.squared, 1)
                    for t in range(NT):
                        act.wait_ge(s.up_ready, t + 1)
                        act.activation(qt[:, t, :, :], pq[:, 0:H * QD].rearrange("p (h d) -> p h d", d=QD),
                                       ACT.Copy).then_inc(s.q_out, 1)
                        act.activation(kt[:, t, :, 0:NOPE], pkv[:].rearrange("p (h d) -> p h d", h=H)[:, :, 0:NOPE],
                                       ACT.Copy).then_inc(s.k_out, 1)
                    for t in range(NT):
                        act.wait_ge(s.qk_turned, t + 1)
                        act.activation(qT[:, :, t * P:(t + 1) * P], pT[0:QD, 2 * (t % 2), :, :], ACT.Copy,
                                       scale=float(QD ** -0.5)).then_inc(s.q_copied, 1)

                @block.vector
                def _(dve):
                    dve.wait_ge(s.loaded, 96)
                    for k in range(2):
                        dve.tensor_scalar(wq[:, k, :], wq[:, k, :], gq[:, k:k + 1], None, ALU.mult).then_inc(s.weighted, 1)
                    dve.tensor_scalar(wkv[:], wkv[:], gkv[:, 0:1], None, ALU.mult).then_inc(s.weighted, 1)
                    dve.wait_ge(s.squared, 1)
                    dve.tensor_scalar(ss[:, 0, :], ss[:, 0, :], 1.0 / QR, EPS, ALU.mult, ALU.add).then_inc(s.meaned, 1)
                    dve.tensor_scalar(ss[:, 1, :], ss[:, 1, :], 1.0 / KVR, EPS, ALU.mult, ALU.add).then_inc(s.meaned, 1)
                    dve.wait_ge(s.rooted, 1)
                    for t in range(NT):
                        dve.tensor_scalar(lat[:, t, 0:QR], lat[:, t, 0:QR], rr[:, 0, t:t + 1], None, ALU.mult)
                        dve.tensor_scalar(lat[:, t, QR:QR + KVR], lat[:, t, QR:QR + KVR], rr[:, 1, t:t + 1], None,
                                          ALU.mult).then_inc(s.normed, 1)
                    for t in range(NT):
                        dve.wait_ge(s.c_turned, t + 1)
                        if t >= 2:
                            dve.wait_ge(s.up_ready, t - 1)
                        dve.tensor_copy(cT[:, t % 2, :, :], pc[:, t % 2, 0:3 * P].rearrange("p (k n) -> p k n", k=3)).then_inc(s.c_copied, 1)
                        if t:
                            dve.wait_ge(s.k_out, t)
                            dve.tensor_copy(v[:, t - 1, :, :], pkv[:].rearrange("p (h d) -> p h d", h=H)[:, :, NOPE:NOPE + HD]).then_inc(s.v_out, 1)
                    dve.wait_ge(s.k_out, NT)
                    dve.tensor_copy(v[:, NT - 1, :, :], pkv[:].rearrange("p (h d) -> p h d", h=H)[:, :, NOPE:NOPE + HD]).then_inc(s.v_out, 1)
                    dve.wait_ge(s.q_out, NT)
                    cos = lambda n: rope[:, :, 0:HR].unsqueeze(2).to_broadcast([P, NT, n, HR])
                    sin = lambda n: rope[:, :, HR:ROPE].unsqueeze(2).to_broadcast([P, NT, n, HR])
                    q1, q2 = qt[:, :, :, NOPE:NOPE + HR], qt[:, :, :, NOPE + HR:QD]
                    kr = lat[:, :, QR + KVR:].unsqueeze(2)
                    for src1, src2, a0, n in ((q1, q2, 0, H), (kr[:, :, :, 0:HR], kr[:, :, :, HR:ROPE], H, 1)):
                        dst = slice(a0, a0 + n)
                        dve.tensor_tensor(t1[:, :, dst, :], src1, cos(n), ALU.mult)
                        dve.tensor_tensor(t2[:, :, dst, :], src2, sin(n), ALU.mult)
                        dve.tensor_tensor(t3[:, :, dst, :], src1, sin(n), ALU.mult)
                        dve.tensor_tensor(t4[:, :, dst, :], src2, cos(n), ALU.mult).then_inc(s.products, 1)
                    dve.wait_ge(s.products, 2)
                    dve.tensor_tensor(q1, t1[:, :, 0:H, :], t2[:, :, 0:H, :], ALU.subtract).then_inc(s.rotated, 1)
                    dve.tensor_tensor(q2, t3[:, :, 0:H, :], t4[:, :, 0:H, :], ALU.add).then_inc(s.rotated, 1)
                    for h in range(H):
                        dve.tensor_tensor(kt[:, :, h, NOPE:NOPE + HR], t1[:, :, H, :], t2[:, :, H, :], ALU.subtract).then_inc(s.rotated, 1)
                        dve.tensor_tensor(kt[:, :, h, NOPE + HR:QD], t3[:, :, H, :], t4[:, :, H, :], ALU.add).then_inc(s.rotated, 1)
                    for t in range(NT):
                        dve.wait_ge(s.qk_turned, t + 1)
                        dve.tensor_copy(kT[:, :, t * P:(t + 1) * P], pT[0:QD, 2 * (t % 2) + 1, :, :]).then_inc(s.k_copied, 1)

                @block.tensor
                def _(pe):
                    def turn(t):
                        pe.wait_ge(s.normed, t + 1)
                        if t >= 2:
                            pe.wait_ge(s.c_copied, t - 1)
                        for k in range(3):
                            mm = pe.transpose(pc[:, t % 2, k * P:(k + 1) * P], lat[:, t, k * P:(k + 1) * P], ident[:])
                        mm.then_inc(s.c_turned, 1)

                    turn(0)
                    pe.wait_ge(s.weighted, 3)
                    for t in range(NT):
                        if t < NT - 1:
                            turn(t + 1)
                        pe.wait_ge(s.c_copied, t + 1)
                        if t:
                            pe.wait_ge(s.q_out, t)
                            pe.wait_ge(s.v_out, t)
                        pe.matmul(pq[:, 0:H * QD], cT[:, t % 2, 0, :], wq[:, 0, :], start=True, stop=False)
                        pe.matmul(pq[:, 0:H * QD], cT[:, t % 2, 1, :], wq[:, 1, :], start=False, stop=True)
                        pe.matmul(pkv[:], cT[:, t % 2, 2, :], wkv[:], start=True, stop=True).then_inc(s.up_ready, 1)
                    pe.wait_ge(s.rotated, 2 + 2 * H)
                    for t in range(NT):
                        if t >= 2:
                            pe.wait_ge(s.q_copied, t - 1)
                            pe.wait_ge(s.k_copied, t - 1)
                        for h in range(H):
                            pe.transpose(pT[0:QD, 2 * (t % 2), h, :], qt[:, t, h, :], ident[:])
                            mm = pe.transpose(pT[0:QD, 2 * (t % 2) + 1, h, :], kt[:, t, h, :], ident[:])
                        mm.then_inc(s.qk_turned, 1)
        items = []
        for i in range(NT):
            for h in range(H):
                keys = (i + 1) * P
                items.append(Item(
                    q=qT[:, h, i * P:(i + 1) * P], k=kT[:, h, 0:keys], n=keys, slope=-1.0,
                    table=mask[:, T - keys:T], v=lambda j, h=h: v[:, j, h, :],
                    gate=None, out=y[:, i, h * HD:(h + 1) * HD], adds=False))
        attend(nc, tag, items, ident)


def attend(nc, tag, items, ident):
    N = len(items)
    chunks = [[(k0, min(k0 + P, it.n)) for k0 in range(0, it.n, P)] for it in items]
    groups = [[ch[a:a + 4] for a in range(0, len(ch), 4)] for ch in chunks]
    first_group = np.cumsum([0] + [len(g) for g in groups]).tolist()
    with ExitStack() as c:
        sb = lambda n, shape: c.enter_context(nc.sbuf_tensor(f"{tag}_{n}", shape, F32))
        S = [sb(f"S{i}", [P, T]) for i in range(2)]
        E = [sb(f"E{i}", [P, T]) for i in range(2)]
        ET = [sb(f"ET{i}", [P, T // P, P]) for i in range(2)]
        nmax, total, factor = sb("nmax", [P, N]), sb("total", [P, N]), sb("factor", [P, N])
        score = c.enter_context(nc.psum_tensor(f"{tag}_score", [P, 2, T], F32))
        turned = c.enter_context(nc.psum_tensor(f"{tag}_turned", [P, 2, 4, P], F32))
        outp = c.enter_context(nc.psum_tensor(f"{tag}_outp", [P, 2, 512], F32))
        s = c.enter_context(phase(nc, "scored", "biased", "max_ready", "exp_ready", "turned", "copied",
                                  "out_ready", "inverted", "factored", "written"))
        with nc.Block() as block:
            @block.tensor
            def _(pe):
                def scores(n):
                    it = items[n]
                    if n >= 2:
                        pe.wait_ge(s.biased, n - 1)
                    for k0 in range(0, it.n, 512):
                        k1 = min(k0 + 512, it.n)
                        mm = pe.matmul(score[:, n % 2, k0:k1], it.q, it.k[:, k0:k1], start=True, stop=True)
                    mm.then_inc(s.scored, 1)

                def turns(n):
                    pe.wait_ge(s.exp_ready, n + 1)
                    for g, group in enumerate(groups[n]):
                        m = first_group[n] + g
                        if m >= 2:
                            pe.wait_ge(s.copied, m - 1)
                        for j, (k0, k1) in enumerate(group):
                            mm = pe.transpose(turned[0:k1 - k0, m % 2, j, :], E[n % 2][:, k0:k1], ident[:])
                        mm.then_inc(s.turned, 1)

                def outs(n):
                    pe.wait_ge(s.copied, first_group[n + 1])
                    if n >= 2:
                        pe.wait_ge(s.written, n - 1)
                    last = len(chunks[n]) - 1
                    for j, (k0, k1) in enumerate(chunks[n]):
                        mm = pe.matmul(outp[:, n % 2, 0:HD], ET[n % 2][0:k1 - k0, j, :], items[n].v(j),
                                       start=(j == 0), stop=(j == last))
                    mm.then_inc(s.out_ready, 1)

                for n in range(N + 2):
                    if n < N:
                        scores(n)
                    if 1 <= n <= N:
                        turns(n - 1)
                    if n >= 2:
                        outs(n - 2)

            @block.vector
            def _(dve):
                def softmax_max(n):
                    it = items[n]
                    dve.wait_ge(s.scored, n + 1)
                    if n >= 2:
                        dve.wait_ge(s.exp_ready, n - 1)
                    sc = S[n % 2][:, 0:it.n]
                    dve.scalar_tensor_tensor(sc, it.table, -it.slope, score[:, n % 2, 0:it.n], ALU.mult,
                                             ALU.add).then_inc(s.biased, 1)
                    dve.wait_ge(s.biased, n + 1)
                    dve.tensor_reduce(nmax[:, n:n + 1], sc, AX.X, ALU.max, negate=True).then_inc(s.max_ready, 1)

                def write(n):
                    it = items[n]
                    dve.wait_ge(s.exp_ready, n + 1)
                    dve.reciprocal(factor[:, n:n + 1], total[:, n:n + 1]).then_inc(s.inverted, 1)
                    dve.wait_ge(s.inverted, n + 1)
                    if it.gate is not None:
                        dve.tensor_tensor(factor[:, n:n + 1], factor[:, n:n + 1], it.gate, ALU.mult).then_inc(s.factored, 1)
                        dve.wait_ge(s.factored, n + 1)
                    dve.wait_ge(s.out_ready, n + 1)
                    if it.adds:
                        dve.wait_ge(s.written, n)
                        dve.scalar_tensor_tensor(it.out, outp[:, n % 2, 0:HD], factor[:, n:n + 1], it.out, ALU.mult,
                                                 ALU.add).then_inc(s.written, 1)
                    else:
                        dve.tensor_scalar(it.out, outp[:, n % 2, 0:HD], factor[:, n:n + 1], None, ALU.mult).then_inc(s.written, 1)

                for n in range(N + 3):
                    if n < N:
                        softmax_max(n)
                    if n >= 3:
                        write(n - 3)

            @block.scalar
            def _(act):
                def exps(n):
                    act.wait_ge(s.max_ready, n + 1)
                    if n >= 2:
                        act.wait_ge(s.turned, first_group[n - 1])
                    act.activation(E[n % 2][:, 0:items[n].n], S[n % 2][:, 0:items[n].n], ACT.Exp, bias=nmax[:, n:n + 1],
                                   accum_out=total[:, n:n + 1]).then_inc(s.exp_ready, 1)

                def copies(n):
                    if n >= 2:
                        act.wait_ge(s.out_ready, n - 1)
                    for g, group in enumerate(groups[n]):
                        m = first_group[n] + g
                        act.wait_ge(s.turned, m + 1)
                        keys = group[0][1] - group[0][0]
                        act.activation(ET[n % 2][0:keys, 4 * g:4 * g + len(group), :], turned[0:keys, m % 2, 0:len(group), :],
                                       ACT.Copy).then_inc(s.copied, 1)

                for n in range(N + 1):
                    if n < N:
                        exps(n)
                    if n:
                        copies(n - 1)


def sparse(nc, tag, proj, tab, w, ident, y):
    NG = T // CMP_STRIDE
    with ExitStack() as c:
        sb = lambda n, shape: c.enter_context(nc.sbuf_tensor(f"{tag}_{n}", shape, F32))
        off = COL["nq"]
        raw = sb("raw", [P, NT, D_IN - off])
        qT = sb("qT", [HD, H, T])
        ksT, kwT = sb("ksT", [HD, T]), sb("kwT", [HD, T])
        dist, dist_win = sb("dist", [P, T]), sb("dist_win", [P, WIN + P])
        dist_cmp, any_cmp = sb("dist_cmp", [P, NT, NCMP]), sb("any_cmp", [P, NT])
        gates = sb("gates", [P, NT, H, 3])
        kcmp, vcmp = sb("kcmp", [HD, NCMP]), sb("vcmp", [NCMP, HD])
        cols = lambda n: raw[:, :, COL[n] - off:COL[n] - off + SPLITS[n]]
        with ExitStack() as c1:
            sb1 = lambda n, shape: c1.enter_context(nc.sbuf_tensor(f"{tag}_{n}", shape, F32))
            ps1 = lambda n, shape: c1.enter_context(nc.psum_tensor(f"{tag}_{n}", shape, F32))
            w1 = sb1("w1", [P, CMP_LEN, CMP_HID])
            w2 = sb1("w2", [P, 2, 2, HD])
            pe_in, peT = sb1("pe_in", [CMP_LEN, P]), sb1("peT", [P, CMP_LEN])
            kvT = sb1("kvT", [P, T])
            u = [sb1(f"u{i}", [P, NG, CMP_STRIDE]) for i in range(2)]
            th, hid = sb1("th", [P, 2, 2, NCMP]), sb1("hid", [P, 2, 2, NCMP])
            pq, pk = ps1("pq", [HD, 2, H, P]), ps1("pk", [P, 2, 4, P])
            ph, pcmp = ps1("ph", [P, 2, 512]), ps1("pcmp", [HD, 2, 512])
            s = c1.enter_context(phase(nc, "raw_loaded", "loaded", "w1_loaded", "turned", "q_copied", "kv_copied",
                                       "pe_turned", "pe_copied", "placed", "hid_ready", "tanh_ready", "hid_done",
                                       "cmp_ready", "gate_tanh", "gated"))
            with nc.Block() as block:
                @block.sync
                def _(sp):
                    sp.dma_start(raw[:], tokens(proj, off, D_IN)).then_inc(s.raw_loaded, 16)
                    for i, n in enumerate("kv"):
                        sp.dma_start(pe_in[:, i * HD:(i + 1) * HD], w[f"cmp_pe_{n}"]).then_inc(s.loaded, 16)
                        sp.dma_start(w2[:, i, :, :], w[f"cmp_w2_{n}"].rearrange("(a p) d -> p a d", p=P)).then_inc(s.loaded, 16)
                    for i, n in enumerate("kv"):
                        sp.dma_start(w1[i * HD:(i + 1) * HD, :, :],
                                     w[f"cmp_w1_{n}"].rearrange("(j d) c -> d j c", d=HD)).then_inc(s.w1_loaded, 16)
                    for dst, name in ((dist, "t_dist"), (dist_win, "t_dist_win"), (dist_cmp, "t_dist_cmp"), (any_cmp, "t_any_cmp")):
                        sp.dma_start(dst[:], tab[name]).then_inc(s.loaded, 16)

                @block.tensor
                def _(pe):
                    pe.wait_ge(s.loaded, 128)
                    pe.wait_ge(s.raw_loaded, 16)
                    pe.transpose(ph[:, 0, 0:CMP_LEN], pe_in[:], ident[0:CMP_LEN, 0:CMP_LEN]).then_inc(s.pe_turned, 1)
                    for t in range(NT):
                        if t >= 2:
                            pe.wait_ge(s.q_copied, t - 1)
                            pe.wait_ge(s.kv_copied, 3 * (t - 1))
                        for h in range(H):
                            pe.transpose(pq[:, t % 2, h, :], raw[:, t, h * HD:(h + 1) * HD], ident[:])
                        pe.transpose(pk[:, t % 2, 0, :], raw[:, t, COL["kc"] - off:COL["ks"] - off], ident[:])
                        pe.transpose(pk[0:HD, t % 2, 1, :], cols("ks")[:, t, :], ident[:])
                        pe.transpose(pk[0:HD, t % 2, 2, :], cols("kw")[:, t, :], ident[:]).then_inc(s.turned, 1)
                    pe.wait_ge(s.w1_loaded, 32)
                    pe.wait_ge(s.placed, 2)
                    pe.wait_ge(s.pe_copied, 1)
                    for i in range(2):
                        half = slice(i * HD, (i + 1) * HD)
                        for a in range(2):
                            for j in range(CMP_LEN):
                                g0 = j // CMP_STRIDE
                                mm = pe.matmul(ph[:, i, a * 64:a * 64 + NCMP], w1[half, j, a * P:(a + 1) * P],
                                               u[g0][half, g0:g0 + NCMP, j % CMP_STRIDE],
                                               start=(j == 0), stop=(j == CMP_LEN - 1))
                        mm.then_inc(s.hid_ready, 1)
                    pe.wait_ge(s.hid_done, 2)
                    for a in range(2):
                        pe.matmul(pcmp[:, 0, 0:NCMP], w2[:, 0, a, :], hid[:, 0, a, :], start=(a == 0), stop=(a == 1))
                    for a in range(2):
                        mm = pe.matmul(pcmp[0:NCMP, 1, 0:HD], hid[:, 1, a, :], w2[:, 1, a, :], start=(a == 0), stop=(a == 1))
                    mm.then_inc(s.cmp_ready, 1)

                @block.scalar
                def _(act):
                    act.wait_ge(s.raw_loaded, 16)
                    act.activation(gates[:].rearrange("p t h b -> p t (h b)"), cols("gate"), ACT.Tanh, scale=0.5).then_inc(s.gate_tanh, 1)
                    for t in range(NT):
                        act.wait_ge(s.turned, t + 1)
                        act.activation(qT[:, :, t * P:(t + 1) * P], pq[:, t % 2, :, :], ACT.Copy, scale=float(HD ** -0.5)).then_inc(s.q_copied, 1)
                    for i in range(2):
                        act.wait_ge(s.hid_ready, i + 1)
                        act.activation(th[:, i, :, :], ph[:, i, 0:P].rearrange("p (a n) -> p a n", a=2)[:, :, 0:NCMP], ACT.Tanh,
                                       scale=0.5).then_inc(s.tanh_ready, 1)
                    act.wait_ge(s.cmp_ready, 1)
                    act.activation(kcmp[:], pcmp[:, 0, 0:NCMP], ACT.Copy, scale=0.5)
                    act.activation(vcmp[:], pcmp[0:NCMP, 1, 0:HD], ACT.Copy, scale=0.5)

                @block.vector
                def _(dve):
                    dve.wait_ge(s.pe_turned, 1)
                    dve.tensor_copy(peT[:], ph[:, 0, 0:CMP_LEN]).then_inc(s.pe_copied, 1)
                    for t in range(NT):
                        here = slice(t * P, (t + 1) * P)
                        dve.wait_ge(s.turned, t + 1)
                        dve.tensor_copy(kvT[:, here], pk[:, t % 2, 0, :]).then_inc(s.kv_copied, 1)
                        dve.tensor_copy(ksT[:, here], pk[0:HD, t % 2, 1, :]).then_inc(s.kv_copied, 1)
                        dve.tensor_copy(kwT[:, here], pk[0:HD, t % 2, 2, :]).then_inc(s.kv_copied, 1)
                    dve.wait_ge(s.kv_copied, 3 * NT)
                    dve.wait_ge(s.pe_copied, 1)
                    for g0 in range(2):
                        dve.tensor_tensor(u[g0][:], kvT[:].rearrange("p (n j) -> p n j", j=CMP_STRIDE),
                                          peT[:, g0 * CMP_STRIDE:(g0 + 1) * CMP_STRIDE].unsqueeze(1).to_broadcast([P, NG, CMP_STRIDE]),
                                          ALU.add).then_inc(s.placed, 1)
                    dve.wait_ge(s.gate_tanh, 1)
                    dve.tensor_scalar(gates[:], gates[:], 0.5, 0.5, ALU.mult, ALU.add).then_inc(s.gated, 1)
                    dve.wait_ge(s.gated, 1)
                    dve.wait_ge(s.loaded, 128)
                    dve.tensor_tensor(gates[:, :, :, 0], gates[:, :, :, 0], any_cmp[:].unsqueeze(2).to_broadcast([P, NT, H]), ALU.mult)
                    for i in range(2):
                        dve.wait_ge(s.tanh_ready, i + 1)
                        dve.scalar_tensor_tensor(hid[:, i, :, :], th[:, i, :, :], 1.0,
                                                 ph[:, i, 0:P].rearrange("p (a n) -> p a n", a=2)[:, :, 0:NCMP],
                                                 ALU.add, ALU.mult).then_inc(s.hid_done, 1)
        items = []
        for i in range(NT):
            for h in range(H):
                base = dict(q=qT[:, h, i * P:(i + 1) * P], slope=SLOPES[h], out=y[:, i, h * HD:(h + 1) * HD])
                keys = (i + 1) * P
                first = max(0, i - WIN // P)
                wkeys = (i + 1 - first) * P
                items.append(Item(**base, k=kcmp[:], n=NCMP, table=dist_cmp[:, i, :], v=lambda j: vcmp[:],
                                             gate=gates[:, i, h, 0:1], adds=False))
                items.append(Item(**base, k=ksT[:, 0:keys], n=keys, table=dist[:, T - keys:T],
                                             v=lambda j: cols("vs")[:, j, :], gate=gates[:, i, h, 1:2], adds=True))
                items.append(Item(**base, k=kwT[:, first * P:keys], n=wkeys, table=dist_win[:, WIN + P - wkeys:],
                                             v=lambda j, first=first: cols("vw")[:, first + j, :],
                                             gate=gates[:, i, h, 2:3], adds=True))
        attend(nc, tag, items, ident)


def hybrid_layers(nc, a, tab, out):
    proj = nc.dram_tensor("projections", (T, D_IN), F32).ap()
    with ExitStack() as c:
        h = c.enter_context(nc.sbuf_tensor("h", [P, NT, D], F32))
        ident = c.enter_context(nc.sbuf_tensor("ident", [P, P], F32))
        with phase(nc, "x_loaded") as s, nc.Block() as block:
            @block.sync
            def _(sp):
                sp.dma_start(h[:], tokens(a["x"][0], 0, D)).then_inc(s.x_loaded, 16)
                sp.dma_start(ident[:], tab["t_ident"]).then_inc(s.x_loaded, 16)
                sp.wait_ge(s.x_loaded, 32)
        layer_norm(nc, "norm_emb", h, a["ln_emb_g"], a["ln_emb_b"])
        with nc.Fori(0, DEPTH) as l:
            w = {n: a[n][l] for n in a if n not in ("x", "ln_emb_g", "ln_emb_b")}
            with ExitStack() as c1:
                hi, lo = (c1.enter_context(nc.sbuf_tensor(n, [P, KT, T], F32R)) for n in ("x_hi", "x_lo"))
                feature_major(nc, "fmx", h, hi, lo, ident)
                project(nc, "in", w["w_in"], D_IN, hi, lo, to_dram=proj)
            with ExitStack() as c1:
                y = c1.enter_context(nc.sbuf_tensor("y", [P, NT, D], F32))
                ssd(nc, "ssd", proj, tab, w, ident, y[:, :, 0:GW])
                latent(nc, "mla", proj, tab, w, ident, y[:, :, GW:2 * GW])
                retention(nc, "ret", proj, tab, ident, y[:, :, 2 * GW:3 * GW])
                sparse(nc, "nsa", proj, tab, w, ident, y[:, :, 3 * GW:4 * GW])
                hi, lo = (c1.enter_context(nc.sbuf_tensor(n, [P, KT, T], F32R)) for n in ("y_hi", "y_lo"))
                feature_major(nc, "fmy", y, hi, lo, ident)
                project(nc, "out", w["w_out"], D, hi, lo, into=h)
            layer_norm(nc, "norm1", h, w["ln1_g"], w["ln1_b"])
            with ExitStack() as c1:
                hi, lo = (c1.enter_context(nc.sbuf_tensor(n, [P, KT, T], F32R)) for n in ("h_hi", "h_lo"))
                feature_major(nc, "fmh", h, hi, lo, ident)
                mlp(nc, w["w_mlp1"], w["w_mlp2"], hi, lo, h)
            layer_norm(nc, "norm2", h, w["ln2_g"], w["ln2_b"])
        with phase(nc, "stored") as s, nc.Block() as block:
            @block.sync
            def _(sp):
                sp.dma_start(tokens(out[0], 0, D), h[:]).then_inc(s.stored, 16)
                sp.wait_ge(s.stored, 16)


_INS = ["x", "ln_emb_g", "ln_emb_b", "w_in", "conv_w", "conv_b", "dt_bias", "a_log", "d_skip", "ssm_norm_g",
        "q_norm_g", "w_uq", "kv_norm_g", "w_ukv", "cmp_pe_k", "cmp_w1_k", "cmp_w2_k", "cmp_pe_v", "cmp_w1_v",
        "cmp_w2_v", "w_out", "ln1_g", "ln1_b", "w_mlp1", "w_mlp2", "ln2_g", "ln2_b"]


def kernel(**inputs):
    import concourse.bacc as bacc
    from concourse.bass_utils import run_bass_kernel_spmd

    nc = bacc.Bacc("TRN2", target_bir_lowering=False, num_devices=1)
    arrays = {n: np.ascontiguousarray(inputs[n]) for n in _INS}
    tables = shape_tables()
    dram = {n: nc.dram_tensor(n, v.shape, F32, kind="ExternalInput").ap() for n, v in (arrays | tables).items()}
    out = nc.dram_tensor("out", (1, T, D), F32, kind="ExternalOutput").ap()
    hybrid_layers(nc, {n: dram[n] for n in arrays}, {n: dram[n] for n in tables}, out)
    r = run_bass_kernel_spmd(nc, [arrays | tables], core_ids=[0])
    return r.results[0]["out"]
```

```python
from collections import namedtuple
from contextlib import ExitStack, contextmanager

import numpy as np

import concourse.bass as bass
from concourse import mybir

F32 = mybir.dt.float32
F32R = mybir.dt.float32r
ACT = mybir.ActivationFunctionType
ALU = mybir.AluOpType
AX = mybir.AxisListType

P = 128
D = 1024
T = 1024
DEPTH = 2
NT = T // P
KT = D // P
GW = D // 4
H = 4
HD = GW // H
STATE = 128
XBC = GW + 2 * 2 * STATE
CONV = 4
QR, KVR, ROPE, NOPE = 256, 128, 32, 64
QD = NOPE + ROPE
DFF = 4 * D
CMP_LEN, CMP_STRIDE, CMP_HID, WIN = 32, 16, 256, 512
NCMP = (T - CMP_LEN) // CMP_STRIDE + 1
EPS = 1e-5
MASKED = -2.0 ** 100
ALPHA = (2.0 * DEPTH) ** 0.25
SLOPES = [2.0 ** (-8.0 * (h + 1) / H) for h in range(H)]

SPLITS = dict(z=GW, xbc=XBC, dt=H, cq=QR, ckv=KVR, kr=ROPE, rq=GW, rk=GW, rv=GW, rg=GW,
              nq=GW, kc=HD, vc=HD, ks=HD, vs=HD, kw=HD, vw=HD, gate=3 * H)
COL = dict(zip(SPLITS, np.cumsum([0] + list(SPLITS.values()))[:-1].tolist()))
D_IN = sum(SPLITS.values())
SLOT = 256
NSLOT = D_IN // SLOT
REST = D_IN - NSLOT * SLOT


Branch = namedtuple("Branch", "width tiles score mask score_T mask_T values ident m_rows")


def shape_tables():
    f = np.float32
    tok = np.arange(T, dtype=f)

    def rope(dim):
        inv = f(10000.0) ** (-np.arange(0, dim, 2, dtype=f) / f(dim))
        ang = (tok[:, None] * inv[None, :]).astype(f)
        return np.concatenate([np.cos(ang), np.sin(ang)], 1).astype(f).reshape(NT, P, dim)

    p = np.arange(P)
    log_gamma = np.log1p(-np.exp2(-5.0 - np.arange(H)))
    diff = (p[None, :] - p[:, None]).astype(np.float64)
    decay = np.where(diff[:, None] >= 0, np.exp(np.maximum(diff, 0)[:, None] * log_gamma[None, :, None]), 0)
    zeta = np.exp((P - 1 - p)[:, None] * log_gamma[None])
    xi = np.exp((p + 1)[:, None] * log_gamma[None])
    scale = HD ** -0.5
    n = np.arange(NCMP + 1)
    qpos = np.arange(T).reshape(NT, P)
    valid = (n * CMP_STRIDE + CMP_LEN - 1 <= qpos[:, :, None]) & (n < NCMP)
    mask_cmp = np.where(valid, 0, MASKED).transpose(1, 0, 2)
    diag, far = (np.where(ok, 0, MASKED) for ok in (p[None, :] <= p[:, None], p[None, :] > p[:, None]))
    slopes = np.array(SLOPES)
    qrows = np.stack([np.broadcast_to(slopes[:, None], (H, NT)), -slopes[:, None] * (np.arange(NT) * P)])
    krows = np.zeros((HD, 3, T))
    for b in range(3):
        krows[H * b:H * b + H, b] = 1
    krows[32, 0, :NCMP + 1] = n * CMP_STRIDE + 0.5 * (CMP_LEN - 1)
    krows[32, 1:] = np.arange(T)
    krows[33] = 1
    pick = np.broadcast_to((np.arange(3 * H)[:, None] % H == np.arange(H))[:, :, None], (3 * H, H, P))
    return {
        "t_ident": np.eye(P, dtype=f),
        "t_upto": (p[:, None] <= p[None, :]).astype(f),
        "t_later": np.where(p[:, None] <= p[None, :], 0, MASKED).astype(f),
        "t_rope_ret": np.ascontiguousarray(rope(HD).transpose(1, 0, 2)),
        "t_rope_mla": np.ascontiguousarray(rope(ROPE).transpose(1, 0, 2)),
        "t_decay": (decay * scale).astype(f),
        "t_zeta": (zeta * scale).astype(f),
        "t_xi": xi.astype(f),
        "t_chunk": np.broadcast_to(np.exp(P * log_gamma), (P, H)).astype(f).copy(),
        "t_masks": np.stack([diag, diag.T, far, far.T], 1).astype(f),
        "t_mask_cmp": mask_cmp.astype(f),
        "t_mask_cmp_T": np.ascontiguousarray(mask_cmp.transpose(2, 1, 0)).astype(f),
        "t_any_cmp": np.ascontiguousarray(valid.any(-1).T).astype(f),
        "t_qrows": qrows.astype(f),
        "t_krows": krows.astype(f),
        "t_pick": pick.astype(f),
    }


@contextmanager
def phase(nc, *names):
    first = min(nc.free_semaphores)
    sems = [nc.alloc_semaphore(n, num=first + i) for i, n in enumerate(names)]
    yield namedtuple("Semaphores", names)(*sems)
    nums = [s.num for s in sems]
    assert max(nums) - min(nums) == len(nums) - 1
    nc.all_engine_barrier(sems_to_clear=range(min(nums), max(nums) + 1))
    for s in sems:
        nc.release_semaphore(s)


def ordered(eng, sem):
    done = [0]

    def step(instruction):
        done[0] += 1
        instruction.then_inc(sem, 1)
        eng.wait_ge(sem, done[0])

    return step


def tokens(ap, c0, c1):
    return ap.rearrange("(t p) c -> p t c", p=P)[:, :, c0:c1]


def tokens_at(ap, c0, n):
    return ap.rearrange("(t p) c -> p t c", p=P)[:, :, bass.ds(c0, n)]


def layer_norm(nc, tag, x, gain, bias):
    with ExitStack() as c:
        sb = lambda n, s: c.enter_context(nc.sbuf_tensor(f"{tag}_{n}", s, F32))
        g, b = sb("g", [P, D]), sb("b", [P, D])
        stats, mv = sb("stats", [P, NT, 2, 6]), sb("mv", [P, NT, 2])
        var, rstd, shift, power = sb("var", [P, NT]), sb("rstd", [P, NT]), sb("shift", [P, NT]), sb("power", [P, NT])
        centre = c.enter_context(nc.psum_tensor(f"{tag}_centre", [P, 4, D], F32))
        s = c.enter_context(phase(nc, "gains_loaded", "power_set", "stats_ready", "moments_ready", "var_ready",
                                  "rstd_ready", "shift_ready", "centred", "scaled"))
        with nc.Block() as block:
            @block.sync
            def _(sp):
                sp.dma_start(g[:], gain.partition_broadcast(P)).then_inc(s.gains_loaded, 16)
                sp.dma_start(b[:], bias.partition_broadcast(P)).then_inc(s.gains_loaded, 16)

            @block.vector
            def _(dve):
                for t in range(NT):
                    for half in range(2):
                        dve.bn_stats(stats[:, t, half, :], x[:, t, half * 512:(half + 1) * 512]).then_inc(s.stats_ready, 1)
                for t in range(NT):
                    dve.wait_ge(s.stats_ready, 2 * t + 2)
                    dve.bn_aggr(mv[:, t, :], stats[:, t, :, :].rearrange("p a b -> p (a b)")).then_inc(s.moments_ready, 1)
                dve.wait_ge(s.moments_ready, NT)
                dve.tensor_scalar(var[:], mv[:, :, 1], EPS, None, ALU.add).then_inc(s.var_ready, 1)
                dve.wait_ge(s.rstd_ready, 1)
                dve.scalar_tensor_tensor(shift[:], mv[:, :, 0], -1.0, rstd[:], ALU.mult, ALU.mult).then_inc(s.shift_ready, 1)
                dve.wait_ge(s.gains_loaded, 32)
                for t in range(NT):
                    dve.wait_ge(s.centred, t + 1)
                    dve.tensor_tensor(x[:, t, :], centre[:, t % 4, :], g[:], ALU.mult).then_inc(s.scaled, 1)
                    if t % 2:
                        dve.wait_ge(s.scaled, t)
                        dve.tensor_tensor(x[:, t - 1, :], x[:, t - 1, :], b[:], ALU.add)

            @block.gpsimd
            def _(pool):
                pool.memset(power[:], -0.5).then_inc(s.power_set, 1)
                pool.wait_ge(s.power_set, 1)
                pool.wait_ge(s.var_ready, 1)
                pool.tensor_tensor(rstd[:], var[:], power[:], ALU.pow).then_inc(s.rstd_ready, 1)
                pool.wait_ge(s.gains_loaded, 32)
                for t in range(1, NT, 2):
                    pool.wait_ge(s.scaled, t + 1)
                    pool.tensor_tensor(x[:, t, :], x[:, t, :], b[:], ALU.add)

            @block.scalar
            def _(act):
                act.wait_ge(s.shift_ready, 1)
                for t in range(NT):
                    if t >= 4:
                        act.wait_ge(s.scaled, t - 3)
                    act.activation(centre[:, t % 4, :], x[:, t, :], ACT.Identity, bias=shift[:, t:t + 1],
                                   scale=rstd[:, t:t + 1]).then_inc(s.centred, 1)


def feature_major(nc, tag, src, hi, lo, ident):
    with ExitStack() as c:
        turned = c.enter_context(nc.psum_tensor(f"{tag}_turned", [P, 8, 4, P], F32))
        s = c.enter_context(phase(nc, "bank_turned", "hi_copied", "lo_copied"))
        groups = [(t, half) for t in range(NT) for half in range(2)]
        with nc.Block() as block:
            @block.tensor
            def _(pe):
                for g, (t, half) in enumerate(groups):
                    if g >= 8:
                        pe.wait_ge(s.lo_copied, g - 7)
                    for j in range(4):
                        k = 4 * half + j
                        mm = pe.transpose(turned[:, g % 8, j, :], src[:, t, k * P:(k + 1) * P], ident[:])
                    mm.then_inc(s.bank_turned, 1)

            @block.scalar
            def _(act):
                for g, (t, half) in enumerate(groups):
                    act.wait_ge(s.bank_turned, g + 1)
                    act.activation(hi[:, 4 * half:4 * half + 4, t * P:(t + 1) * P], turned[:, g % 8, :, :],
                                   ACT.Copy).then_inc(s.hi_copied, 1)

            @block.vector
            def _(dve):
                for g, (t, half) in enumerate(groups):
                    dve.wait_ge(s.hi_copied, g + 1)
                    dst = slice(4 * half, 4 * half + 4), slice(t * P, (t + 1) * P)
                    dve.tensor_tensor(lo[:, dst[0], dst[1]], turned[:, g % 8, :, :],
                                      hi[:, dst[0], dst[1]].bitcast(F32), ALU.subtract).then_inc(s.lo_copied, 1)


def weight_slot(w, c0, n):
    return w.rearrange("(k p) c -> p k c", p=P)[:, :, bass.ds(c0, n)]


def project(nc, tag, w, cols, hi, lo, to_dram=None, into=None):
    full, rest = cols // SLOT, cols % SLOT
    assert full % 2 == 0
    with ExitStack() as c:
        raw = c.enter_context(nc.sbuf_tensor(f"{tag}_raw", [P, 2, KT, SLOT], F32))
        whi = [c.enter_context(nc.sbuf_tensor(f"{tag}_whi{i}", [P, KT, SLOT], F32R)) for i in range(2)]
        wlo = [c.enter_context(nc.sbuf_tensor(f"{tag}_wlo{i}", [P, KT, SLOT], F32R)) for i in range(2)]
        acc = c.enter_context(nc.psum_tensor(f"{tag}_acc", [P, 8, 512], F32))
        if to_dram is not None:
            stage = c.enter_context(nc.sbuf_tensor(f"{tag}_stage", [P, 2, NT, SLOT], F32))
        s = c.enter_context(phase(nc, "raw_loaded0", "raw_loaded1", "whi_ready", "wlo_ready",
                                  "acc_ready", "acc_free", "stage_full", "stored0", "stored1"))
        loaded, stored = [s.raw_loaded0, s.raw_loaded1], [s.stored0, s.stored1]
        n_slots = full + (1 if rest else 0)

        with nc.Block() as block:
            @block.sync
            def _(sp):
                def load(n, b, width, first=False):
                    if not first:
                        sp.wait_ge(s.wlo_ready, n - 1)
                    sp.dma_start(raw[:, b, :, 0:width], weight_slot(w, n * SLOT, width)).then_inc(loaded[b], 16)

                def store(n, b, width):
                    sp.wait_ge(s.stage_full, n * NT + NT)
                    sp.dma_start(tokens_at(to_dram, n * SLOT, width), stage[:, b, :, 0:width]).then_inc(stored[b], 16)

                load(0, 0, SLOT, first=True)
                load(1, 1, SLOT, first=True)
                with sp.Fori(0, full // 2 - 1) as i:
                    for b in range(2):
                        load(2 * i + b + 2, b, SLOT)
                        if to_dram is not None:
                            store(2 * i + b, b, SLOT)
                if rest:
                    load(full, 0, rest)
                if to_dram is not None:
                    store(full - 2, 0, SLOT)
                    store(full - 1, 1, SLOT)
                    if rest:
                        store(full, 0, rest)
                    sp.wait_ge(stored[0], 16 * ((n_slots + 1) // 2))
                    sp.wait_ge(stored[1], 16 * (n_slots // 2))

            @block.scalar
            def _(act):
                def split_hi(n, b, turn, width, first=False):
                    act.wait_ge(loaded[b], 16 * turn + 16)
                    if not first:
                        act.wait_ge(s.acc_ready, n * NT - NT)
                    act.activation(whi[b][:, :, 0:width], raw[:, b, :, 0:width], ACT.Copy).then_inc(s.whi_ready, 1)

                def copy_out(n, b, turn, width):
                    act.wait_ge(stored[b], 16 * turn)
                    for t in range(NT):
                        act.wait_ge(s.acc_ready, n * NT + t + 1)
                        act.activation(stage[:, b, t, 0:width], acc[:, t, 0:width], ACT.Copy).then_inc(s.stage_full, 1)

                split_hi(0, 0, 0, SLOT, first=True)
                split_hi(1, 1, 0, SLOT, first=True)
                if to_dram is None:
                    for n in range(2, n_slots):
                        split_hi(n, n % 2, n // 2, SLOT)
                    return
                for b in range(2):
                    for t in range(NT):
                        act.wait_ge(s.acc_ready, b * NT + t + 1)
                        act.activation(stage[:, b, t, :], acc[:, t, 0:SLOT], ACT.Copy).then_inc(s.stage_full, 1)
                    split_hi(b + 2, b, 1, SLOT)
                with act.Fori(1, full // 2 - 1) as i:
                    for b in range(2):
                        copy_out(2 * i + b, b, i, SLOT)
                        split_hi(2 * i + b + 2, b, i + 1, SLOT)
                i = full // 2 - 1
                copy_out(full - 2, 0, i, SLOT)
                if rest:
                    split_hi(full, 0, i + 1, rest)
                copy_out(full - 1, 1, i, SLOT)
                if rest:
                    copy_out(full, 0, i + 1, rest)

            @block.vector
            def _(dve):
                def split_lo(n, b, width):
                    dve.wait_ge(s.whi_ready, n + 1)
                    dve.tensor_tensor(wlo[b][:, :, 0:width], raw[:, b, :, 0:width],
                                      whi[b][:, :, 0:width].bitcast(F32), ALU.subtract).then_inc(s.wlo_ready, 1)
                def add_in(n):
                    for t in range(NT):
                        dve.wait_ge(s.acc_ready, n * NT + t + 1)
                        here = into[:, t, n * SLOT:(n + 1) * SLOT]
                        dve.scalar_tensor_tensor(here, here, ALPHA, acc[:, t, 0:SLOT], ALU.mult,
                                                 ALU.add).then_inc(s.acc_free, 1)

                split_lo(0, 0, SLOT)
                if to_dram is None:
                    for n in range(n_slots):
                        if n + 1 < n_slots:
                            split_lo(n + 1, (n + 1) % 2, SLOT)
                        add_in(n)
                    return
                split_lo(1, 1, SLOT)
                with dve.Fori(1, full // 2) as i:
                    for b in range(2):
                        split_lo(2 * i + b, b, SLOT)
                if rest:
                    split_lo(full, 0, rest)

            @block.tensor
            def _(pe):
                free = s.acc_free if to_dram is None else s.stage_full

                def slot(n, b, width, first=False):
                    pe.wait_ge(s.wlo_ready, n + 1)
                    for t in range(NT):
                        if not first:
                            pe.wait_ge(free, n * NT + t - NT + 1)
                        out = acc[:, t, 0:width]
                        for k in range(KT):
                            xh, xl = hi[:, k, t * P:(t + 1) * P], lo[:, k, t * P:(t + 1) * P]
                            pe.matmul(out, xh, whi[b][:, k, 0:width], start=(k == 0), stop=False)
                            pe.matmul(out, xh, wlo[b][:, k, 0:width], start=False, stop=False)
                            mm = pe.matmul(out, xl, whi[b][:, k, 0:width], start=False, stop=(k == KT - 1))
                        mm.then_inc(s.acc_ready, 1)

                if to_dram is None:
                    for n in range(n_slots):
                        slot(n, n % 2, SLOT, first=(n == 0))
                    return
                slot(0, 0, SLOT, first=True)
                slot(1, 1, SLOT)
                with pe.Fori(1, full // 2) as i:
                    for b in range(2):
                        slot(2 * i + b, b, SLOT)
                if rest:
                    slot(full, 0, rest)




def mlp(nc, w1, w2, hi, lo, h):
    FF = 2 * P
    G = DFF // FF
    with ExitStack() as c:
        raw1 = c.enter_context(nc.sbuf_tensor("mlp_raw1", [P, KT, FF], F32))
        raw2 = c.enter_context(nc.sbuf_tensor("mlp_raw2", [P, 2, D], F32))
        w1hi = c.enter_context(nc.sbuf_tensor("mlp_w1hi", [P, KT, FF], F32R))
        w1lo = c.enter_context(nc.sbuf_tensor("mlp_w1lo", [P, KT, FF], F32R))
        w2hi = c.enter_context(nc.sbuf_tensor("mlp_w2hi", [P, 2, D], F32R))
        w2lo = c.enter_context(nc.sbuf_tensor("mlp_w2lo", [P, 2, D], F32R))
        ahi = [c.enter_context(nc.sbuf_tensor(f"mlp_ahi{i}", [P, 2, T], F32R)) for i in range(2)]
        alo = [c.enter_context(nc.sbuf_tensor(f"mlp_alo{i}", [P, 2, T], F32R)) for i in range(2)]
        relu = c.enter_context(nc.sbuf_tensor("mlp_relu", [P, 2, 512], F32))
        square = c.enter_context(nc.sbuf_tensor("mlp_square", [P, 2, 512], F32))
        hid = c.enter_context(nc.psum_tensor("mlp_hid", [P, 4, 512], F32))
        out = c.enter_context(nc.psum_tensor("mlp_out", [P, 4, 512], F32))
        s = c.enter_context(phase(nc, "w1_loaded", "w2_loaded", "w1hi_ready", "w1lo_ready", "w2hi_ready",
                                  "w2lo_ready", "hid_ready", "relu_ready", "square_ready", "ahi_ready",
                                  "alo_ready", "out_ready", "added", "scaled"))
        w1_v = w1.rearrange("(k p) f -> p k f", p=P)
        w2_v = w2.rearrange("(g j p) c -> g p j c", p=P, j=2)
        HB, OB = 4, 2 * NT

        with nc.Block() as block:
            @block.sync
            def _(sp):
                def load1(g):
                    sp.dma_start(raw1[:], w1_v[:, :, bass.ds(g * FF, FF)]).then_inc(s.w1_loaded, 16)

                def load2(g):
                    sp.dma_start(raw2[:], w2_v[g, :, :, :]).then_inc(s.w2_loaded, 16)

                load1(0)
                load2(0)
                with sp.Fori(1, G) as g:
                    sp.wait_ge(s.w1lo_ready, g)
                    load1(g)
                    sp.wait_ge(s.w2lo_ready, g)
                    load2(g)

            @block.scalar
            def _(act):
                def split1(g, first=False):
                    act.wait_ge(s.w1_loaded, 16 * g + 16)
                    if not first:
                        act.wait_ge(s.hid_ready, HB * g)
                    act.activation(w1hi[:], raw1[:], ACT.Copy).then_inc(s.w1hi_ready, 1)

                def split2(g, first=False):
                    act.wait_ge(s.w2_loaded, 16 * g + 16)
                    if not first:
                        act.wait_ge(s.out_ready, OB * g)
                    act.activation(w2hi[:], raw2[:], ACT.Copy).then_inc(s.w2hi_ready, 1)

                def hidden(g, buf, first=False):
                    for n in range(HB + 1):
                        if n < HB:
                            act.wait_ge(s.hid_ready, HB * g + n + 1)
                            if not first or n >= 2:
                                act.wait_ge(s.square_ready, HB * g + n - 1)
                            act.activation(relu[:, n % 2, :], hid[:, n, :], ACT.Relu).then_inc(s.relu_ready, 1)
                        if n:
                            j, half = (n - 1) // 2, (n - 1) % 2
                            act.wait_ge(s.square_ready, HB * g + n)
                            act.activation(ahi[buf][:, j, half * 512:(half + 1) * 512], square[:, (n - 1) % 2, :],
                                           ACT.Copy).then_inc(s.ahi_ready, 1)

                split1(0, first=True)
                hidden(0, 0, first=True)
                split1(1)
                split2(0, first=True)
                hidden(1, 1)
                split1(2)
                split2(1)
                hidden(2, 0)
                split1(3)
                with act.Fori(1, G // 2 - 1) as i:
                    for b in range(2):
                        g = 2 * i + b + 1
                        split2(g - 1)
                        hidden(g, (b + 1) % 2)
                        split1(g + 1)
                split2(G - 2)
                hidden(G - 1, 1)
                split2(G - 1)

            @block.vector
            def _(dve):
                def split1(g):
                    dve.wait_ge(s.w1hi_ready, g + 1)
                    dve.tensor_tensor(w1lo[:], raw1[:], w1hi[:].bitcast(F32), ALU.subtract).then_inc(s.w1lo_ready, 1)

                def split2(g):
                    dve.wait_ge(s.w2hi_ready, g + 1)
                    dve.tensor_tensor(w2lo[:], raw2[:], w2hi[:].bitcast(F32), ALU.subtract).then_inc(s.w2lo_ready, 1)

                def hidden(g, buf, first=False):
                    for n in range(HB + 1):
                        if n < HB:
                            dve.wait_ge(s.relu_ready, HB * g + n + 1)
                            if not first or n >= 2:
                                dve.wait_ge(s.ahi_ready, HB * g + n - 1)
                                dve.wait_ge(s.alo_ready, HB * g + n - 1)
                            dve.tensor_tensor(square[:, n % 2, :], relu[:, n % 2, :], relu[:, n % 2, :],
                                              ALU.mult).then_inc(s.square_ready, 1)
                        if n:
                            j, half = (n - 1) // 2, (n - 1) % 2
                            part = slice(half * 512, (half + 1) * 512)
                            dve.wait_ge(s.ahi_ready, HB * g + n)
                            dve.tensor_tensor(alo[buf][:, j, part], square[:, (n - 1) % 2, :],
                                              ahi[buf][:, j, part].bitcast(F32), ALU.subtract).then_inc(s.alo_ready, 1)

                def add_out(g, first=False):
                    if not first:
                        dve.wait_ge(s.added, OB * g)
                    for m in range(OB):
                        t, half = m // 2, m % 2
                        part = h[:, t, half * 512:(half + 1) * 512]
                        dve.wait_ge(s.out_ready, OB * g + m + 1)
                        dve.tensor_tensor(part, part, out[:, m % 4, :], ALU.add).then_inc(s.added, 1)

                split1(0)
                dve.tensor_scalar(h[:], h[:], ALPHA, None, ALU.mult).then_inc(s.scaled, 1)
                hidden(0, 0, first=True)
                split1(1)
                dve.wait_ge(s.scaled, 1)
                split2(0)
                hidden(1, 1)
                split1(2)
                add_out(0, first=True)
                split2(1)
                hidden(2, 0)
                split1(3)
                add_out(1)
                with dve.Fori(1, G // 2 - 1) as i:
                    for b in range(2):
                        g = 2 * i + b + 1
                        split2(g - 1)
                        hidden(g, (b + 1) % 2)
                        split1(g + 1)
                        add_out(g - 1)
                split2(G - 2)
                hidden(G - 1, 1)
                add_out(G - 2)
                split2(G - 1)
                add_out(G - 1)

            @block.tensor
            def _(pe):
                def up(g, first=False):
                    pe.wait_ge(s.w1lo_ready, g + 1)
                    for n in range(HB):
                        j, half = n // 2, n % 2
                        if not first:
                            pe.wait_ge(s.relu_ready, HB * (g - 1) + n + 1)
                        for k in range(KT):
                            wh, wl = w1hi[:, k, j * P:(j + 1) * P], w1lo[:, k, j * P:(j + 1) * P]
                            xh, xl = hi[:, k, half * 512:(half + 1) * 512], lo[:, k, half * 512:(half + 1) * 512]
                            pe.matmul(hid[:, n, :], wh, xh, start=(k == 0), stop=False)
                            pe.matmul(hid[:, n, :], wh, xl, start=False, stop=False)
                            mm = pe.matmul(hid[:, n, :], wl, xh, start=False, stop=(k == KT - 1))
                        mm.then_inc(s.hid_ready, 1)

                def down(g, buf, first=False):
                    pe.wait_ge(s.w2lo_ready, g + 1)
                    pe.wait_ge(s.alo_ready, HB * g + HB)
                    for m in range(OB):
                        t, half = m // 2, m % 2
                        if not first or m >= 4:
                            pe.wait_ge(s.added, OB * g + m - 3)
                        for j in range(2):
                            xh, xl = ahi[buf][:, j, t * P:(t + 1) * P], alo[buf][:, j, t * P:(t + 1) * P]
                            wh, wl = w2hi[:, j, half * 512:(half + 1) * 512], w2lo[:, j, half * 512:(half + 1) * 512]
                            pe.matmul(out[:, m % 4, :], xh, wh, start=(j == 0), stop=False)
                            pe.matmul(out[:, m % 4, :], xh, wl, start=False, stop=False)
                            mm = pe.matmul(out[:, m % 4, :], xl, wh, start=False, stop=(j == 1))
                        mm.then_inc(s.out_ready, 1)

                up(0, first=True)
                up(1)
                down(0, 0, first=True)
                up(2)
                down(1, 1)
                with pe.Fori(1, G // 2 - 1) as i:
                    for b in range(2):
                        g = 2 * i + b + 1
                        up(g)
                        down(g - 1, b)
                up(G - 1)
                down(G - 2, 0)
                down(G - 1, 1)


def retention(nc, tag, proj, tab, ident, y):
    with ExitStack() as c:
        sb = lambda n, shape: c.enter_context(nc.sbuf_tensor(f"{tag}_{n}", shape, F32))
        ps = lambda n, shape: c.enter_context(nc.psum_tensor(f"{tag}_{n}", shape, F32))
        qkvg = sb("qkvg", [P, NT, 4 * GW])
        rope, decay = sb("rope", [P, NT, HD]), sb("decay", [P, H, P])
        zeta, xi, chunk = sb("zeta", [P, H]), sb("xi", [P, H]), sb("chunk", [P, H])
        qk = sb("qk", [P, NT, 2 * H, HD])
        t1, t2 = sb("t1", [P, NT, 2 * H, HD // 2]), sb("t2", [P, NT, 2 * H, HD // 2])
        t3, t4 = sb("t3", [P, NT, 2 * H, HD // 2]), sb("t4", [P, NT, 2 * H, HD // 2])
        zv = sb("zv", [P, NT, H, HD])
        qT, kT = sb("qT", [HD, H, P]), sb("kT", [HD, H, P])
        sc, cross = sb("sc", [P, H, P]), sb("cross", [P, H, HD])
        state = sb("state", [HD, H, HD])
        sq, ss, rr = sb("sq", [P, NT * H, HD]), sb("ss", [P, NT * H]), sb("rr", [P, NT * H])
        sg, power = sb("sg", [P, NT, GW]), sb("power", [P, NT * H])
        psq, psk = ps("psq", [HD, H, P]), ps("psk", [HD, H, P])
        pss, psy = ps("pss", [P, H, P]), ps("psy", [P, 512])
        psx, pskv = ps("psx", [P, 512]), ps("pskv", [HD, 512])
        s = c.enter_context(phase(nc, "loaded", "tables", "products", "rotated", "zv_ready", "turned", "q_copied",
                                  "k_copied", "scored", "decayed", "y_ready", "crossed", "y_out", "kv_ready",
                                  "state_decayed", "state_ready", "squared", "summed", "meaned", "rooted",
                                  "tanh_ready", "gated", "gate_mul", "normed", "power_set"))
        yv = y.rearrange("p t (h d) -> p t h d", d=HD)
        q_in = qkvg[:, :, 0:2 * GW].rearrange("p t (h d) -> p t h d", d=HD)
        x1, x2 = q_in[:, :, :, 0:HD // 2], q_in[:, :, :, HD // 2:HD]
        cos = rope[:, :, 0:HD // 2].unsqueeze(2).to_broadcast([P, NT, 2 * H, HD // 2])
        sin = rope[:, :, HD // 2:HD].unsqueeze(2).to_broadcast([P, NT, 2 * H, HD // 2])
        v = qkvg[:, :, 2 * GW:3 * GW].rearrange("p t (h d) -> p t h d", d=HD)
        g = qkvg[:, :, 3 * GW:4 * GW]

        with nc.Block() as block:
            @block.sync
            def _(sp):
                sp.dma_start(qkvg[:], tokens(proj, COL["rq"], COL["rq"] + 4 * GW)).then_inc(s.loaded, 16)
                sp.dma_start(rope[:], tab["t_rope_ret"]).then_inc(s.tables, 16)
                sp.dma_start(decay[:], tab["t_decay"]).then_inc(s.tables, 16)
                sp.dma_start(zeta[:], tab["t_zeta"]).then_inc(s.tables, 16)
                sp.dma_start(xi[:], tab["t_xi"]).then_inc(s.tables, 16)
                sp.dma_start(chunk[:], tab["t_chunk"]).then_inc(s.tables, 16)

            @block.gpsimd
            def _(pool):
                pool.memset(power[:], -0.5).then_inc(s.power_set, 1)
                pool.wait_ge(s.loaded, 16)
                pool.wait_ge(s.tables, 80)
                pool.tensor_tensor(t3[:], x1, sin, ALU.mult).then_inc(s.products, 1)
                pool.tensor_tensor(t4[:], x2, cos, ALU.mult).then_inc(s.products, 1)
                pool.wait_ge(s.power_set, 1)
                pool.wait_ge(s.meaned, 1)
                pool.tensor_tensor(rr[:], ss[:], power[:], ALU.pow).then_inc(s.rooted, 1)

            @block.vector
            def _(dve):
                dve.wait_ge(s.loaded, 16)
                dve.wait_ge(s.tables, 80)
                dve.tensor_tensor(t1[:], x1, cos, ALU.mult)
                dve.tensor_tensor(t2[:], x2, sin, ALU.mult).then_inc(s.products, 1)
                dve.tensor_tensor(zv[:], v, zeta[:].unsqueeze(1).unsqueeze(3).to_broadcast([P, NT, H, HD]),
                                  ALU.mult).then_inc(s.zv_ready, 1)
                dve.wait_ge(s.products, 3)
                dve.tensor_tensor(qk[:, :, :, 0:HD // 2], t1[:], t2[:], ALU.subtract).then_inc(s.rotated, 1)
                dve.tensor_tensor(qk[:, :, :, HD // 2:HD], t3[:], t4[:], ALU.add).then_inc(s.rotated, 1)
                for t in range(NT):
                    dve.wait_ge(s.turned, t + 1)
                    if t:
                        dve.wait_ge(s.scored, t)
                        dve.wait_ge(s.y_ready, t)
                    dve.tensor_copy(kT[:], psk[:]).then_inc(s.k_copied, 1)
                    dve.wait_ge(s.scored, t + 1)
                    dve.tensor_tensor(sc[:], pss[:], decay[:], ALU.mult).then_inc(s.decayed, 1)
                    dve.wait_ge(s.y_ready, t + 1)
                    if t:
                        xib = xi[:].unsqueeze(2).to_broadcast([P, H, HD])
                        dve.tensor_tensor(cross[:], psx[:, 0:GW].rearrange("p (h d) -> p h d", d=HD), xib,
                                          ALU.mult).then_inc(s.crossed, 1)
                        dve.wait_ge(s.crossed, t)
                        dve.tensor_tensor(yv[:, t, :, :], cross[:], psy[:, 0:GW].rearrange("p (h d) -> p h d", d=HD),
                                          ALU.add).then_inc(s.y_out, 1)
                        if t < NT - 1:
                            dve.wait_ge(s.state_ready, t)
                            dve.tensor_tensor(state[:], state[:], chunk[0:HD, :].unsqueeze(2).to_broadcast([HD, H, HD]),
                                              ALU.mult).then_inc(s.state_decayed, 1)
                            dve.wait_ge(s.state_decayed, t)
                            dve.wait_ge(s.kv_ready, t + 1)
                            dve.tensor_tensor(state[:], state[:], pskv[:, 0:GW].rearrange("p (h d) -> p h d", d=HD),
                                              ALU.add).then_inc(s.state_ready, 1)
                    else:
                        dve.tensor_copy(yv[:, t, :, :], psy[:, 0:GW].rearrange("p (h d) -> p h d", d=HD)).then_inc(s.y_out, 1)
                        dve.wait_ge(s.kv_ready, 1)
                        dve.tensor_copy(state[:], pskv[:, 0:GW].rearrange("p (h d) -> p h d", d=HD)).then_inc(s.state_ready, 1)
                dve.wait_ge(s.squared, 1)
                dve.tensor_reduce(ss[:], sq[:], AX.X, ALU.add).then_inc(s.summed, 1)
                dve.wait_ge(s.tanh_ready, 1)
                dve.tensor_scalar(sg[:], sg[:], 0.5, 0.5, ALU.mult, ALU.add).then_inc(s.gated, 1)
                dve.wait_ge(s.summed, 1)
                dve.tensor_scalar(ss[:], ss[:], 1.0 / HD, EPS, ALU.mult, ALU.add).then_inc(s.meaned, 1)
                dve.wait_ge(s.gated, 1)
                dve.tensor_tensor(sg[:], sg[:], g, ALU.mult).then_inc(s.gate_mul, 1)
                dve.wait_ge(s.rooted, 1)
                dve.wait_ge(s.y_out, NT)
                yh = y.rearrange("p t (h d) -> p t h d", d=HD)
                dve.tensor_tensor(yh, yh, rr[:].rearrange("p (t h) -> p t h", h=H).unsqueeze(3).to_broadcast([P, NT, H, HD]),
                                  ALU.mult).then_inc(s.normed, 1)
                dve.wait_ge(s.normed, 1)
                dve.wait_ge(s.gate_mul, 1)
                dve.tensor_tensor(y, y, sg[:], ALU.mult)

            @block.scalar
            def _(act):
                act.wait_ge(s.loaded, 16)
                act.activation(sg[:], g, ACT.Tanh, scale=0.5).then_inc(s.tanh_ready, 1)
                for t in range(NT):
                    act.wait_ge(s.turned, t + 1)
                    if t:
                        act.wait_ge(s.y_ready, t)
                    act.activation(qT[:], psq[:], ACT.Copy).then_inc(s.q_copied, 1)
                act.wait_ge(s.y_out, NT)
                act.activation(sq[:].rearrange("p (t h) d -> p t h d", h=H), yv, ACT.Square).then_inc(s.squared, 1)

            @block.tensor
            def _(pe):
                def turn(t):
                    if t:
                        pe.wait_ge(s.q_copied, t)
                        pe.wait_ge(s.k_copied, t)
                    for h in range(H):
                        pe.transpose(psq[:, h, :], qk[:, t, h, :], ident[:])
                        mm = pe.transpose(psk[:, h, :], qk[:, t, H + h, :], ident[:])
                    mm.then_inc(s.turned, 1)

                pe.wait_ge(s.rotated, 2)
                turn(0)
                for t in range(NT):
                    pe.wait_ge(s.q_copied, t + 1)
                    pe.wait_ge(s.k_copied, t + 1)
                    if t:
                        pe.wait_ge(s.decayed, t)
                    for h in range(H):
                        mm = pe.matmul(pss[:, h, :], kT[:, h, :], qT[:, h, :], start=True, stop=True)
                    mm.then_inc(s.scored, 1)
                    if t < NT - 1:
                        turn(t + 1)
                    pe.wait_ge(s.zv_ready, 1)
                    if t:
                        pe.wait_ge(s.state_ready, t)
                    if t < NT - 1:
                        for h in range(H):
                            mm = pe.matmul(pskv[:, h * HD:(h + 1) * HD], qk[:, t, H + h, :], zv[:, t, h, :],
                                           start=True, stop=True)
                        mm.then_inc(s.kv_ready, 1)
                    if t:
                        pe.wait_ge(s.y_out, t)
                        for h in range(H):
                            pe.matmul(psx[:, h * HD:(h + 1) * HD], qT[:, h, :], state[:, h, :], start=True, stop=True)
                    pe.wait_ge(s.decayed, t + 1)
                    for h in range(H):
                        mm = pe.matmul(psy[:, h * HD:(h + 1) * HD], sc[:, h, :], v[:, t, h, :], start=True, stop=True)
                    mm.then_inc(s.y_ready, 1)


def ssd(nc, tag, proj, tab, w, ident, y):
    NC = XBC // P
    with ExitStack() as c:
        sb = lambda n, shape: c.enter_context(nc.sbuf_tensor(f"{tag}_{n}", shape, F32))
        ps = lambda n, shape: c.enter_context(nc.psum_tensor(f"{tag}_{n}", shape, F32))
        z, xbc, dtr = sb("z", [P, NT, GW]), sb("xbc", [P, NT, XBC]), sb("dtr", [P, NT, H])
        upto, later, ones = sb("upto", [P, P]), sb("later", [P, P]), sb("ones", [P, P])
        cw, cb = sb("cw", [P, NC, CONV]), sb("cb", [P, NC])
        dtb, alog, skip, gain = sb("dtb", [P, H]), sb("alog", [P, H]), sb("skip", [P, H]), sb("gain", [P, GW])
        xT = sb("xT", [P, NC, T + CONV - 1])
        th = sb("th", [P, T])
        xc = sb("xc", [P, NC, T])
        xb = sb("xb", [P, NT, 2 * GW])
        u, v1, v2, v3, v4 = (sb(n, [P, NT, H]) for n in ("u", "v1", "v2", "v3", "v4"))
        dt, a, acs, eacs, tot, etot, dend = (sb(n, [P, NT, H]) for n in ("dt", "a", "acs", "eacs", "tot", "etot", "dend"))
        nega = sb("nega", [P, H])
        xdt, xdd = sb("xdt", [P, NT, H, HD]), sb("xdd", [P, NT, H, HD])
        E, m = sb("E", [P, H, P]), sb("m", [P, H, P])
        off = sb("off", [P, H, HD])
        state = sb("state", [STATE, H, HD])
        ss, rr, power = sb("ss", [P, NT]), sb("rr", [P, NT]), sb("power", [P, NT])
        bank = [ps(f"bank{i}", [P, 512]) for i in range(8)]
        s = c.enter_context(phase(nc, "xbc_loaded", "loaded", "consts", "halved", "x_turned", "x_copied", "conv_step", "conv_done",
                                  "tanh_done", "silu_done", "b_turned", "b_copied", "dt_step", "dt_exp", "dt_ready",
                                  "a_exp", "a_neg", "a_ready", "sums_ready", "sums_copied", "exps_ready", "dend_ready",
                                  "xdt_ready", "xdd_ready", "rows_ready", "cb_ready", "e_step", "e_ready", "m_ready",
                                  "diag_ready", "y_step", "y_out", "new_ready", "state_step", "state_ready",
                                  "z_tanh", "gate_step", "squared", "meaned", "rooted", "power_set"))
        yv = y.rearrange("p t (h d) -> p t h d", d=HD)
        xh = xb[:, :, 0:GW].rearrange("p t (h d) -> p t h d", d=HD)
        per = lambda ap: ap.unsqueeze(3).to_broadcast([P, NT, H, HD])
        heads = lambda ap: ap[:, 0:GW].rearrange("p (h d) -> p h d", d=HD)
        bc = lambda ap: ap.unsqueeze(1).to_broadcast([P, NT, H])

        with nc.Block() as block:
            @block.sync
            def _(sp):
                sp.dma_start(xbc[:], tokens(proj, COL["xbc"], COL["xbc"] + XBC)).then_inc(s.xbc_loaded, 16)
                with nc.allow_non_contiguous_dma(reason="a few KB of conv weights, turned"):
                    for k in range(CONV):
                        sp.dma_start(cw[:, :, k], w["conv_w"][k].rearrange("(c p) -> p c", p=P)).then_inc(s.consts, 16)
                    sp.dma_start(cb[:], w["conv_b"].rearrange("(c p) -> p c", p=P)).then_inc(s.consts, 16)
                sp.dma_start(dtr[:], tokens(proj, COL["dt"], COL["dt"] + H)).then_inc(s.loaded, 16)
                sp.dma_start(dtb[:], w["dt_bias"].partition_broadcast(P)).then_inc(s.loaded, 16)
                sp.dma_start(alog[:], w["a_log"].partition_broadcast(P)).then_inc(s.loaded, 16)
                sp.dma_start(skip[:], w["d_skip"].partition_broadcast(P)).then_inc(s.loaded, 16)
                sp.dma_start(gain[:], w["ssm_norm_g"].partition_broadcast(P)).then_inc(s.loaded, 16)
                sp.dma_start(upto[:], tab["t_upto"]).then_inc(s.loaded, 16)
                sp.dma_start(later[:], tab["t_later"]).then_inc(s.loaded, 16)
                sp.dma_start(z[:], tokens(proj, COL["z"], COL["z"] + GW)).then_inc(s.loaded, 16)

            @block.gpsimd
            def _(pool):
                pool.memset(ones[:], 1.0).then_inc(s.power_set, 1)
                pool.memset(xT[:, :, 0:CONV - 1], 0.0).then_inc(s.power_set, 1)
                pool.memset(power[:], -0.5).then_inc(s.power_set, 1)
                pool.wait_ge(s.b_copied, NT)
                pool.wait_ge(s.dt_ready, 1)
                pool.tensor_tensor(xdt[:], xh, per(dt[:]), ALU.mult).then_inc(s.xdt_ready, 1)
                pool.wait_ge(s.dend_ready, 1)
                pool.wait_ge(s.xdt_ready, 1)
                pool.tensor_tensor(xdd[:], xdt[:], per(dend[:]), ALU.mult).then_inc(s.xdd_ready, 1)
                pool.tensor_tensor(yv, xh, skip[:].unsqueeze(1).unsqueeze(3).to_broadcast([P, NT, H, HD]),
                                   ALU.mult).then_inc(s.xdd_ready, 1)
                pool.wait_ge(s.meaned, 1)
                pool.wait_ge(s.power_set, 3)
                pool.tensor_tensor(rr[:], ss[:], power[:], ALU.pow).then_inc(s.rooted, 1)

            @block.tensor
            def _(pe):
                pe.wait_ge(s.xbc_loaded, 16)
                for n in range(2 * NC):
                    ch, half = n // 2, n % 2
                    if n >= 4:
                        pe.wait_ge(s.x_copied, n - 3)
                    for j in range(4):
                        mm = pe.transpose(bank[4 + n % 4][:, j * P:(j + 1) * P], xbc[:, 4 * half + j, ch * P:(ch + 1) * P], ident[:])
                    mm.then_inc(s.x_turned, 1)
                pe.wait_ge(s.a_ready, 1)
                pe.wait_ge(s.x_copied, 2 * NC)
                pe.wait_ge(s.power_set, 1)
                af = a[:].rearrange("p t h -> p (t h)")
                pe.matmul(bank[4][:, 0:NT * H], upto[:], af, start=True, stop=True)
                pe.matmul(bank[4][:, NT * H:2 * NT * H], ones[:], af, start=True, stop=True,
                          skip_group_check=True).then_inc(s.sums_ready, 1)
                pe.wait_ge(s.silu_done, 4)
                pe.wait_ge(s.sums_copied, 1)
                for t in range(NT):
                    if t >= 2:
                        pe.wait_ge(s.b_copied, t - 1)
                    for j in range(4):
                        mm = pe.transpose(bank[6 + t % 2][:, j * P:(j + 1) * P], xc[:, j, t * P:(t + 1) * P], ident[:])
                    mm.then_inc(s.b_turned, 1)

                def rows(t):
                    if t:
                        pe.wait_ge(s.e_step, 2 * t)
                    else:
                        pe.wait_ge(s.silu_done, NC)
                        pe.wait_ge(s.b_copied, NT)
                    for h in range(H):
                        mm = pe.matmul(bank[0][:, h * P:(h + 1) * P], a[:, t, h:h + 1].to_broadcast([P, P]), upto[:],
                                       start=True, stop=True)
                    mm.then_inc(s.rows_ready, 1)

                rows(0)
                for t in range(NT):
                    here = slice(t * P, (t + 1) * P)
                    if t:
                        pe.wait_ge(s.m_ready, t)
                    for g in range(2):
                        mm = pe.matmul(bank[1][:, g * P:(g + 1) * P], xc[:, 2 + g, here], xc[:, 4 + g, here],
                                       start=True, stop=True)
                    mm.then_inc(s.cb_ready, 1)
                    if t < NT - 1:
                        rows(t + 1)
                        pe.wait_ge(s.xdd_ready, 1)
                        if t:
                            pe.wait_ge(s.state_ready, t)
                        for g in range(2):
                            mm = pe.matmul(bank[4][:, g * P:(g + 1) * P], xb[:, t, GW + g * P:GW + (g + 1) * P],
                                           xdd[:, t, 2 * g:2 * g + 2, :], start=True, stop=True)
                        mm.then_inc(s.new_ready, 1)
                    if t:
                        pe.wait_ge(s.state_ready, t)
                        pe.wait_ge(s.y_out, t)
                        for g in range(2):
                            pe.matmul(bank[3][:, g * P:(g + 1) * P], xc[:, 4 + g, here], state[:, 2 * g:2 * g + 2, :],
                                      start=True, stop=True)
                    pe.wait_ge(s.m_ready, t + 1)
                    for h in range(H):
                        mm = pe.matmul(bank[2][:, h * HD:(h + 1) * HD], m[:, h, :], xdt[:, t, h, :], start=True, stop=True)
                    mm.then_inc(s.diag_ready, 1)

            @block.scalar
            def _(act):
                for n in range(2 * NC):
                    ch, half = n // 2, n % 2
                    act.wait_ge(s.x_turned, n + 1)
                    act.activation(xT[:, ch, CONV - 1 + half * 512:CONV - 1 + (half + 1) * 512], bank[4 + n % 4][:],
                                   ACT.Copy).then_inc(s.x_copied, 1)
                act.wait_ge(s.loaded, 128)
                act.activation(nega[:], alog[:], ACT.Exp).then_inc(s.a_exp, 1)
                act.wait_ge(s.dt_step, 2)
                act.activation(u[:], v2[:], ACT.Exp).then_inc(s.dt_exp, 1)
                for ch in range(NC):
                    act.wait_ge(s.conv_done, ch + 1)
                    if ch:
                        act.wait_ge(s.silu_done, ch)
                    b = 2 * (ch % 2)
                    for half in range(2):
                        i = act.activation(th[:, half * 512:(half + 1) * 512], bank[b + half][:], ACT.Tanh)
                    i.then_inc(s.tanh_done, 1)
                    if ch == 1:
                        act.wait_ge(s.sums_copied, 1)
                        act.activation(eacs[:], acs[:], ACT.Exp)
                        act.activation(etot[:], tot[:], ACT.Exp).then_inc(s.exps_ready, 1)
                        act.activation(dend[:], v4[:], ACT.Exp).then_inc(s.dend_ready, 1)
                for t in range(NT):
                    act.wait_ge(s.b_turned, t + 1)
                    act.activation(xb[:, t, :], bank[6 + t % 2][:], ACT.Copy).then_inc(s.b_copied, 1)
                for t in range(NT):
                    act.wait_ge(s.e_step, 2 * t + 2)
                    act.activation(E[:], E[:], ACT.Exp).then_inc(s.e_ready, 1)
                act.activation(th[:].rearrange("p (a b) -> p a b", a=4), z[:, 0:4, :], ACT.Tanh, scale=0.5).then_inc(s.z_tanh, 1)
                act.wait_ge(s.gate_step, 1)
                act.activation(th[:].rearrange("p (a b) -> p a b", a=4), z[:, 4:8, :], ACT.Tanh, scale=0.5).then_inc(s.z_tanh, 1)
                act.wait_ge(s.gate_step, 4)
                for t in range(NT):
                    i = act.activation(xbc[:, t, 0:GW], y[:, t, :], ACT.Square, accum_out=ss[:, t:t + 1])
                i.then_inc(s.squared, 1)

            @block.vector
            def _(dve):
                dve.wait_ge(s.loaded, 128)
                n = [0]

                def step(i):
                    n[0] += 1
                    i.then_inc(s.dt_step, 1)
                    dve.wait_ge(s.dt_step, n[0])

                step(dve.tensor_tensor(v1[:], dtr[:], bc(dtb[:]), ALU.add))
                step(dve.scalar_tensor_tensor(v2[:], v1[:], -1.0, v1[:], ALU.mult, ALU.min))
                step(dve.tensor_scalar(v1[:], v1[:], 0.0, None, ALU.max))
                dve.wait_ge(s.dt_exp, 1)
                step(dve.tensor_scalar(v2[:], u[:], 2.0, None, ALU.add))
                step(dve.reciprocal(v3[:], v2[:]))
                step(dve.tensor_tensor(u[:], u[:], v3[:], ALU.mult))
                step(dve.tensor_tensor(v2[:], u[:], u[:], ALU.mult))
                step(dve.tensor_scalar(v3[:], v2[:], 1.0 / 17, None, ALU.mult))
                for k in range(7, 0, -1):
                    step(dve.scalar_tensor_tensor(v3[:], v3[:], 1.0 / (2 * k + 1), v2[:], ALU.add, ALU.mult))
                step(dve.scalar_tensor_tensor(v3[:], v3[:], 1.0, u[:], ALU.add, ALU.mult))
                step(dve.scalar_tensor_tensor(dt[:], v3[:], 2.0, v1[:], ALU.mult, ALU.add))
                dve.wait_ge(s.a_exp, 1)
                dve.scalar_tensor_tensor(a[:], dt[:], -1.0, bc(nega[:]), ALU.mult, ALU.mult).then_inc(s.a_ready, 1)
                dve.sem_inc(s.dt_ready, 1)
                dve.wait_ge(s.consts, 80)
                dve.tensor_scalar(cw[:], cw[:], 0.5, None, ALU.mult).then_inc(s.halved, 1)
                dve.tensor_scalar(cb[:], cb[:], 0.5, None, ALU.mult).then_inc(s.halved, 1)
                dve.wait_ge(s.halved, 2)
                dve.wait_ge(s.power_set, 2)
                st = 0
                for ch in range(NC):
                    dve.wait_ge(s.x_copied, 2 * ch + 2)
                    b = 2 * (ch % 2)
                    for k in range(CONV):
                        if k:
                            dve.wait_ge(s.conv_step, st)
                        for half in range(2):
                            src = xT[:, ch, k + half * 512:k + half * 512 + 512]
                            acc = bank[b + half][:]
                            if k == 0:
                                i = dve.tensor_scalar(acc, src, cw[:, ch, 0:1], cb[:, ch:ch + 1], ALU.mult, ALU.add)
                            else:
                                i = dve.scalar_tensor_tensor(acc, src, cw[:, ch, k:k + 1], acc, ALU.mult, ALU.add)
                        if k < CONV - 1:
                            st += 1
                            i.then_inc(s.conv_step, 1)
                    i.then_inc(s.conv_done, 1)
                    dve.wait_ge(s.tanh_done, ch + 1)
                    dve.wait_ge(s.conv_done, ch + 1)
                    for half in range(2):
                        i = dve.scalar_tensor_tensor(xc[:, ch, half * 512:(half + 1) * 512], th[:, half * 512:(half + 1) * 512], 1.0,
                                                     bank[b + half][:], ALU.add, ALU.mult)
                    i.then_inc(s.silu_done, 1)
                    if ch == 0:
                        dve.wait_ge(s.sums_ready, 1)
                        dve.tensor_copy(acs[:], bank[4][:, 0:NT * H].rearrange("p (t h) -> p t h", h=H)).then_inc(s.state_step, 1)
                        dve.tensor_copy(tot[:], bank[4][:, NT * H:2 * NT * H].rearrange("p (t h) -> p t h", h=H)).then_inc(s.state_step, 1)
                        dve.wait_ge(s.state_step, 2)
                        dve.tensor_tensor(v4[:], tot[:], acs[:], ALU.subtract).then_inc(s.sums_copied, 1)

                def expo(t):
                    dve.wait_ge(s.rows_ready, t + 1)
                    if t:
                        dve.wait_ge(s.m_ready, t)
                    dve.tensor_tensor(E[:], bank[0][:].rearrange("p (h l) -> p h l", h=H),
                                      acs[:, t, :].unsqueeze(2).to_broadcast([P, H, P]), ALU.subtract).then_inc(s.e_step, 1)
                    dve.wait_ge(s.e_step, 2 * t + 1)
                    dve.tensor_tensor(E[:], E[:], later[:].unsqueeze(1).to_broadcast([P, H, P]), ALU.add).then_inc(s.e_step, 1)

                expo(0)
                for t in range(NT):
                    dve.wait_ge(s.e_ready, t + 1)
                    dve.wait_ge(s.cb_ready, t + 1)
                    if t:
                        dve.wait_ge(s.diag_ready, t)
                    dve.tensor_tensor(m[:].rearrange("p (g r) l -> p g r l", g=2), E[:].rearrange("p (g r) l -> p g r l", g=2),
                                      bank[1][:, 0:2 * P].rearrange("p (g l) -> p g l", g=2).unsqueeze(2).to_broadcast([P, 2, 2, P]),
                                      ALU.mult).then_inc(s.m_ready, 1)
                    if t < NT - 1:
                        expo(t + 1)
                    dve.wait_ge(s.diag_ready, t + 1)
                    dve.wait_ge(s.xdd_ready, 2)
                    if t:
                        dve.wait_ge(s.exps_ready, 1)
                        dve.tensor_tensor(off[:], heads(bank[3]), eacs[:, t, :].unsqueeze(2).to_broadcast([P, H, HD]),
                                          ALU.mult).then_inc(s.y_step, 1)
                        dve.wait_ge(s.y_step, 2 * t - 1)
                        dve.tensor_tensor(off[:], off[:], heads(bank[2]), ALU.add).then_inc(s.y_step, 1)
                        dve.wait_ge(s.y_step, 2 * t)
                        dve.tensor_tensor(yv[:, t, :, :], yv[:, t, :, :], off[:], ALU.add).then_inc(s.y_out, 1)
                    else:
                        dve.tensor_tensor(yv[:, t, :, :], yv[:, t, :, :], heads(bank[2]), ALU.add).then_inc(s.y_out, 1)
                    if t < NT - 1:
                        dve.wait_ge(s.new_ready, t + 1)
                        if t:
                            dve.wait_ge(s.state_ready, t)
                            dve.tensor_tensor(state[:], state[:], etot[:, t, :].unsqueeze(2).to_broadcast([P, H, HD]),
                                              ALU.mult).then_inc(s.state_step, 1)
                            dve.wait_ge(s.state_step, t + 2)
                            dve.tensor_tensor(state[:], state[:], heads(bank[4]), ALU.add).then_inc(s.state_ready, 1)
                        else:
                            dve.tensor_copy(state[:], heads(bank[4])).then_inc(s.state_ready, 1)
                dve.wait_ge(s.y_out, NT)
                for i in range(2):
                    dve.wait_ge(s.z_tanh, i + 1)
                    zi, yi = z[:, 4 * i:4 * i + 4, :], y[:, 4 * i:4 * i + 4, :]
                    dve.scalar_tensor_tensor(zi, th[:].rearrange("p (a b) -> p a b", a=4), 1.0, zi, ALU.add,
                                             ALU.mult).then_inc(s.gate_step, 1)
                    dve.wait_ge(s.gate_step, 2 * i + 1)
                    dve.scalar_tensor_tensor(yi, zi, 0.5, yi, ALU.mult, ALU.mult).then_inc(s.gate_step, 1)
                dve.wait_ge(s.squared, 1)
                dve.tensor_scalar(ss[:], ss[:], 1.0 / GW, EPS, ALU.mult, ALU.add).then_inc(s.meaned, 1)
                dve.wait_ge(s.rooted, 1)
                for t in range(NT):
                    dve.scalar_tensor_tensor(y[:, t, :], y[:, t, :], rr[:, t:t + 1], gain[:], ALU.mult, ALU.mult)


def latent(nc, tag, proj, tab, w, ident, y):
    with ExitStack() as c:
        sb = lambda n, shape: c.enter_context(nc.sbuf_tensor(f"{tag}_{n}", shape, F32))
        sbr = lambda n, shape: c.enter_context(nc.sbuf_tensor(f"{tag}_{n}", shape, F32R))
        qT, kT = sb("qT", [QD + H, H, T]), sb("kT", [QD + H, H, T])
        masks, identr = sbr("masks", [P, 2, P]), sbr("identr", [P, P])
        v, pick = sb("v", [P, NT, H, HD + 1]), sb("pick", [H, H, P])
        with ExitStack() as c1:
            sb1 = lambda n, shape: c1.enter_context(nc.sbuf_tensor(f"{tag}_{n}", shape, F32))
            ps1 = lambda n, shape: c1.enter_context(nc.psum_tensor(f"{tag}_{n}", shape, F32))
            lat = sb1("lat", [P, NT, QR + KVR + ROPE])
            rope = sb1("rope", [P, NT, ROPE])
            wq, wkv = sb1("wq", [P, 2, H * QD]), sb1("wkv", [P, H * (NOPE + HD)])
            gq, gkv = sb1("gq", [P, 2]), sb1("gkv", [P, 1])
            junk, ss, rr, power = sb1("junk", [P, NT, QR + KVR]), sb1("ss", [P, 2, NT]), sb1("rr", [P, 2, NT]), sb1("power", [P, 2, NT])
            cT = sb1("cT", [P, 2, 3, P])
            qt, kt = sb1("qt", [P, NT, H, QD]), sb1("kt", [P, NT, H, QD])
            HR = ROPE // 2
            t1, t2, t3, t4 = (sb1(f"t{i}", [P, NT, H + 1, HR]) for i in range(4))
            pc, pq, pkv = ps1("pc", [P, 2, 512]), ps1("pq", [P, 512]), ps1("pkv", [P, 512])
            pT = ps1("pT", [P, 4, H, P])
            masks_in = sb1("masks_in", [P, 2, P])
            s = c1.enter_context(phase(nc, "lat_loaded", "loaded", "squared", "meaned", "rooted", "power_set", "weighted",
                                       "normed", "c_turned", "c_copied", "up_ready", "q_out", "k_out", "v_out",
                                       "products", "rotated", "qk_turned", "q_copied", "k_copied", "pool_step"))
            x = lambda ap, r: ap[:, :, :, r]
            with nc.Block() as block:
                @block.sync
                def _(sp):
                    sp.dma_start(lat[:], tokens(proj, COL["cq"], COL["rq"])).then_inc(s.lat_loaded, 16)
                    sp.dma_start(wq[:], w["w_uq"].rearrange("(k p) n -> p k n", p=P)).then_inc(s.loaded, 16)
                    sp.dma_start(wkv[:], w["w_ukv"]).then_inc(s.loaded, 16)
                    with nc.allow_non_contiguous_dma(reason="384 gains, one per partition"):
                        sp.dma_start(gq[:], w["q_norm_g"].rearrange("(k p) -> p k", p=P)).then_inc(s.loaded, 16)
                        sp.dma_start(gkv[:], w["kv_norm_g"].rearrange("(k p) -> p k", p=P)).then_inc(s.loaded, 16)
                    sp.dma_start(rope[:], tab["t_rope_mla"]).then_inc(s.loaded, 16)
                    sp.dma_start(masks_in[:], tab["t_masks"][:, 0:2, :]).then_inc(s.loaded, 16)
                    sp.dma_start(pick[:], tab["t_pick"][0:H]).then_inc(s.loaded, 16)

                @block.gpsimd
                def _(pool):
                    step = ordered(pool, s.pool_step)
                    pool.memset(power[:], -0.5).then_inc(s.power_set, 1)
                    pool.wait_ge(s.power_set, 1)
                    pool.memset(v[:], 1.0).then_inc(s.power_set, 1)
                    pool.wait_ge(s.power_set, 2)
                    step(pool.memset(qT[QD:QD + H, :, :], 0.0))
                    step(pool.memset(kT[QD:QD + H, :, :], 1.0))
                    pool.wait_ge(s.loaded, 112)
                    step(pool.tensor_copy(masks[:], masks_in[:]))
                    step(pool.tensor_copy(identr[:], ident[:]))
                    pool.wait_ge(s.power_set, 1)
                    pool.wait_ge(s.meaned, 2)
                    pool.tensor_tensor(rr[:], ss[:], power[:], ALU.pow).then_inc(s.rooted, 1)

                @block.scalar
                def _(act):
                    act.wait_ge(s.lat_loaded, 16)
                    for t in range(NT):
                        act.activation(junk[:, t, 0:QR], lat[:, t, 0:QR], ACT.Square, accum_out=ss[:, 0, t:t + 1])
                        i = act.activation(junk[:, t, QR:QR + KVR], lat[:, t, QR:QR + KVR], ACT.Square, accum_out=ss[:, 1, t:t + 1])
                    i.then_inc(s.squared, 1)
                    for t in range(NT):
                        act.wait_ge(s.up_ready, t + 1)
                        act.activation(qt[:, t, :, :], pq[:, 0:H * QD].rearrange("p (h d) -> p h d", d=QD),
                                       ACT.Copy).then_inc(s.q_out, 1)
                        act.activation(kt[:, t, :, 0:NOPE], pkv[:].rearrange("p (h d) -> p h d", h=H)[:, :, 0:NOPE],
                                       ACT.Copy).then_inc(s.k_out, 1)
                    for t in range(NT):
                        act.wait_ge(s.qk_turned, t + 1)
                        here = slice(t * P, (t + 1) * P)
                        act.activation(qT[0:QD, :, here], pT[0:QD, 2 * (t % 2), :, :], ACT.Copy,
                                       scale=float(QD ** -0.5)).then_inc(s.q_copied, 1)

                @block.vector
                def _(dve):
                    dve.wait_ge(s.loaded, 112)
                    dve.wait_ge(s.power_set, 2)
                    for k in range(2):
                        dve.tensor_scalar(wq[:, k, :], wq[:, k, :], gq[:, k:k + 1], None, ALU.mult).then_inc(s.weighted, 1)
                    dve.tensor_scalar(wkv[:], wkv[:], gkv[:, 0:1], None, ALU.mult).then_inc(s.weighted, 1)
                    dve.wait_ge(s.squared, 1)
                    dve.tensor_scalar(ss[:, 0, :], ss[:, 0, :], 1.0 / QR, EPS, ALU.mult, ALU.add).then_inc(s.meaned, 1)
                    dve.tensor_scalar(ss[:, 1, :], ss[:, 1, :], 1.0 / KVR, EPS, ALU.mult, ALU.add).then_inc(s.meaned, 1)
                    dve.wait_ge(s.rooted, 1)
                    for t in range(NT):
                        dve.tensor_scalar(lat[:, t, 0:QR], lat[:, t, 0:QR], rr[:, 0, t:t + 1], None, ALU.mult)
                        dve.tensor_scalar(lat[:, t, QR:QR + KVR], lat[:, t, QR:QR + KVR], rr[:, 1, t:t + 1], None,
                                          ALU.mult).then_inc(s.normed, 1)
                    for t in range(NT):
                        dve.wait_ge(s.c_turned, t + 1)
                        if t >= 2:
                            dve.wait_ge(s.up_ready, t - 1)
                        dve.tensor_copy(cT[:, t % 2, :, :], pc[:, t % 2, 0:3 * P].rearrange("p (k n) -> p k n", k=3)).then_inc(s.c_copied, 1)
                        if t:
                            dve.wait_ge(s.k_out, t)
                            dve.tensor_copy(v[:, t - 1, :, 0:HD], pkv[:].rearrange("p (h d) -> p h d", h=H)[:, :, NOPE:NOPE + HD]).then_inc(s.v_out, 1)
                    dve.wait_ge(s.k_out, NT)
                    dve.tensor_copy(v[:, NT - 1, :, 0:HD], pkv[:].rearrange("p (h d) -> p h d", h=H)[:, :, NOPE:NOPE + HD]).then_inc(s.v_out, 1)
                    dve.wait_ge(s.q_out, NT)
                    cos = lambda n: rope[:, :, 0:HR].unsqueeze(2).to_broadcast([P, NT, n, HR])
                    sin = lambda n: rope[:, :, HR:ROPE].unsqueeze(2).to_broadcast([P, NT, n, HR])
                    q1, q2 = qt[:, :, :, NOPE:NOPE + HR], qt[:, :, :, NOPE + HR:QD]
                    kr = lat[:, :, QR + KVR:].unsqueeze(2)
                    for src1, src2, a0, n in ((q1, q2, 0, H), (kr[:, :, :, 0:HR], kr[:, :, :, HR:ROPE], H, 1)):
                        dst = slice(a0, a0 + n)
                        dve.tensor_tensor(t1[:, :, dst, :], src1, cos(n), ALU.mult)
                        dve.tensor_tensor(t2[:, :, dst, :], src2, sin(n), ALU.mult)
                        dve.tensor_tensor(t3[:, :, dst, :], src1, sin(n), ALU.mult)
                        dve.tensor_tensor(t4[:, :, dst, :], src2, cos(n), ALU.mult).then_inc(s.products, 1)
                    dve.wait_ge(s.products, 2)
                    dve.tensor_tensor(q1, t1[:, :, 0:H, :], t2[:, :, 0:H, :], ALU.subtract).then_inc(s.rotated, 1)
                    dve.tensor_tensor(q2, t3[:, :, 0:H, :], t4[:, :, 0:H, :], ALU.add).then_inc(s.rotated, 1)
                    for h in range(H):
                        dve.tensor_tensor(kt[:, :, h, NOPE:NOPE + HR], t1[:, :, H, :], t2[:, :, H, :], ALU.subtract).then_inc(s.rotated, 1)
                        dve.tensor_tensor(kt[:, :, h, NOPE + HR:QD], t3[:, :, H, :], t4[:, :, H, :], ALU.add).then_inc(s.rotated, 1)
                    for t in range(NT):
                        here = slice(t * P, (t + 1) * P)
                        dve.wait_ge(s.qk_turned, t + 1)
                        dve.tensor_copy(kT[0:QD, :, here], pT[0:QD, 2 * (t % 2) + 1, :, :]).then_inc(s.k_copied, 1)

                @block.tensor
                def _(pe):
                    def turn(t):
                        pe.wait_ge(s.normed, t + 1)
                        if t >= 2:
                            pe.wait_ge(s.c_copied, t - 1)
                        for k in range(3):
                            mm = pe.transpose(pc[:, t % 2, k * P:(k + 1) * P], lat[:, t, k * P:(k + 1) * P], ident[:])
                        mm.then_inc(s.c_turned, 1)

                    turn(0)
                    pe.wait_ge(s.weighted, 3)
                    for t in range(NT):
                        if t < NT - 1:
                            turn(t + 1)
                        pe.wait_ge(s.c_copied, t + 1)
                        if t:
                            pe.wait_ge(s.q_out, t)
                            pe.wait_ge(s.v_out, t)
                        pe.matmul(pq[:, 0:H * QD], cT[:, t % 2, 0, :], wq[:, 0, :], start=True, stop=False)
                        pe.matmul(pq[:, 0:H * QD], cT[:, t % 2, 1, :], wq[:, 1, :], start=False, stop=True)
                        pe.matmul(pkv[:], cT[:, t % 2, 2, :], wkv[:], start=True, stop=True).then_inc(s.up_ready, 1)
                    pe.wait_ge(s.rotated, 2 + 2 * H)
                    for t in range(NT):
                        if t >= 2:
                            pe.wait_ge(s.q_copied, t - 1)
                            pe.wait_ge(s.k_copied, t - 1)
                        for h in range(H):
                            pe.transpose(pT[0:QD, 2 * (t % 2), h, :], qt[:, t, h, :], ident[:])
                            mm = pe.transpose(pT[0:QD, 2 * (t % 2) + 1, h, :], kt[:, t, h, :], ident[:])
                        mm.then_inc(s.qk_turned, 1)

        def score(i, h, a, z):
            return qT[:, h, i * P:(i + 1) * P], kT[:, h, a * P:(z + 1) * P]

        def score_T(i, kt, out):
            here, keys = slice(i * P, (i + 1) * P), slice(kt * P, (kt + 1) * P)
            passes = []
            for h in range(H):
                passes.append((out[:, h, :], kT[:, h, keys], qT[:, h, here], h == 0, True))
            return passes

        attend(nc, tag, y, [Branch(
            P, lambda i: list(range(i + 1)), score, lambda i, kt: masks[:, 0, :] if kt == i else None,
            score_T, lambda i, kt: masks[:, 1, :] if kt == i else None, lambda kt, h: v[:, kt, h, :], identr,
            lambda i: qT[QD:QD + H, :, i * P:(i + 1) * P])], ident, pick[:], None)


def attend(nc, tag, y, branches, ident, pick, gates):
    NB = len(branches)
    R = NB * H
    pieces = [[] for _ in range(NT)]
    for i in range(NT):
        for b, br in enumerate(branches):
            tiles = br.tiles(i)
            for part in range(0, len(tiles), 4):
                some = tiles[part:part + 4]
                fit = 1 << ((512 // (len(some) * br.width)).bit_length() - 1)
                for h0 in range(0, H, min(fit, H)):
                    pieces[i].append((b, some, h0, min(fit, H), part // 4))
    piece0 = np.cumsum([0] + [len(p) for p in pieces]).tolist()
    steps = [(i, b, j, kt) for i in range(NT) for b in range(NB) for j, kt in enumerate(branches[b].tiles(i))]
    last_of_tile = {n for n in range(len(steps)) if n + 1 == len(steps) or steps[n + 1][0] != steps[n][0]}

    with ExitStack() as c:
        sb = lambda n, shape: c.enter_context(nc.sbuf_tensor(f"{tag}_{n}", shape, F32))
        ps = lambda n, shape: c.enter_context(nc.psum_tensor(f"{tag}_{n}", shape, F32))
        PT = sb("PT", [P, 3, H, P])
        parts, negm = sb("parts", [P, 2, R, 2]), sb("negm", [P, 2, R])
        sums, scaled = sb("sums", [P, 2, H]), sb("scaled", [P, 2, H, HD])
        S, ST = ps("S", [P, 3, 512]), ps("ST", [P, 2, H, P])
        outp, mT = ps("outp", [P, 2, 512]), ps("mT", [P, 512])
        s = c.enter_context(phase(nc, "parts_set", "scored", "part_max", "max_ready", "m_turned", "m_placed", "scored_T",
                                  "exp_ready", "valued", "inverted", "factored", "scaled_ready", "written"))
        with nc.Block() as block:
            @block.gpsimd
            def _(pool):
                pool.memset(parts[:], 3e38).then_inc(s.parts_set, 1)

            @block.tensor
            def _(pe):
                def maxima(i):
                    for m, (b, some, h0, nh, part) in enumerate(pieces[i], piece0[i]):
                        if m >= 3:
                            pe.wait_ge(s.part_max, m - 2)
                        br = branches[b]
                        w = len(some) * br.width
                        for h in range(nh):
                            out = S[:, m % 3, h * w:(h + 1) * w]
                            masked = [(a, kt) for a, kt in enumerate(some) if br.mask(i, kt) is not None]
                            mm = pe.matmul(out, *br.score(i, h0 + h, some[0], some[-1]), start=True, stop=True)
                            for a, kt in masked:
                                mm = pe.matmul(out[:, a * br.width:(a + 1) * br.width], br.ident[:, :], br.mask(i, kt),
                                               start=False, stop=True, skip_group_check=True)
                        mm.then_inc(s.scored, 1)

                def turn_maxima(i):
                    pe.wait_ge(s.max_ready, i + 1)
                    if i:
                        pe.wait_ge(s.m_placed, i)
                    pe.transpose(mT[0:R, 0:P], negm[:, i % 2, :], ident[:]).then_inc(s.m_turned, 1)

                def score_T(n):
                    i, b, j, kt = steps[n]
                    br = branches[b]
                    pe.wait_ge(s.m_placed, i + 1)
                    if n >= 2:
                        pe.wait_ge(s.exp_ready, n - 1)
                    mask = br.mask_T(i, kt)
                    for out, lhsT, rhs, start, stop in br.score_T(i, kt, ST[0:br.width, n % 2, :, :]):
                        mm = pe.matmul(out, lhsT, rhs, start=start, stop=stop and mask is None, skip_group_check=True)
                    if mask is not None:
                        mm = pe.matmul(ST[0:br.width, n % 2, :, :], br.ident[0:br.width, 0:br.width],
                                       mask.unsqueeze(1).to_broadcast([br.width, H, P]), start=False, stop=True,
                                       skip_group_check=True)
                    mm.then_inc(s.scored_T, 1)

                def values(n):
                    i, b, j, kt = steps[n]
                    br = branches[b]
                    m = i * NB + b
                    pe.wait_ge(s.exp_ready, n + 1)
                    if j == 0 and m >= 2:
                        pe.wait_ge(s.written, m - 1)
                    last = len(br.tiles(i)) - 1
                    for h in range(H):
                        mm = pe.matmul(outp[:, m % 2, h * (HD + 1):(h + 1) * (HD + 1)], PT[0:br.width, n % 3, h, :],
                                       br.values(kt, h), start=(j == 0 and h == 0), stop=(j == last), skip_group_check=True)
                    mm.then_inc(s.valued, 1)

                maxima(0)
                turn_maxima(0)
                for n in range(len(steps) + 1):
                    if n < len(steps):
                        i = steps[n][0]
                        more = i + 1 < NT
                        first, last = n == 0 or steps[n - 1][0] != i, n in last_of_tile
                        if last and not first and more:
                            turn_maxima(i + 1)
                        score_T(n)
                    if n:
                        values(n - 1)
                    if n < len(steps) and first and more:
                        maxima(i + 1)
                        if last:
                            turn_maxima(i + 1)

            @block.scalar
            def _(act):
                for n, (i, b, j, kt) in enumerate(steps):
                    act.wait_ge(s.scored_T, n + 1)
                    if n >= 3:
                        act.wait_ge(s.valued, n - 2)
                    w = branches[b].width
                    act.activation(PT[0:w, n % 3, :, :], ST[0:w, n % 2, :, :], ACT.Exp).then_inc(s.exp_ready, 1)

            @block.vector
            def _(dve):
                def maxima(i):
                    for m, (b, some, h0, nh, part) in enumerate(pieces[i], piece0[i]):
                        w = len(some) * branches[b].width
                        dve.wait_ge(s.scored, m + 1)
                        dve.tensor_reduce(parts[:, i % 2, b * H + h0:b * H + h0 + nh, part],
                                          S[:, m % 3, 0:nh * w].rearrange("p (h k) -> p h k", h=nh), AX.X, ALU.max,
                                          negate=True).then_inc(s.part_max, 1)
                    dve.wait_ge(s.part_max, piece0[i + 1])
                    if i >= 2:
                        dve.wait_ge(s.m_turned, i - 1)
                    dve.tensor_reduce(negm[:, i % 2, :], parts[:, i % 2, :, :], AX.X, ALU.min).then_inc(s.max_ready, 1)

                def place(i):
                    dve.wait_ge(s.m_turned, i + 1)
                    dve.tensor_tensor(branches[0].m_rows(i), mT[0:R, 0:P].unsqueeze(1).to_broadcast([R, H, P]), pick,
                                      ALU.mult).then_inc(s.m_placed, 1)

                done = np.cumsum([len(branches[b].tiles(i)) for i in range(NT) for b in range(NB)]).tolist()

                def write(i, b):
                    m = i * NB + b
                    dve.wait_ge(s.valued, done[m])
                    out = outp[:, m % 2, 0:H * (HD + 1)].rearrange("p (h d) -> p h d", h=H)
                    f = sums[:, m % 2, :]
                    dve.reciprocal(f, out[:, :, HD]).then_inc(s.inverted, 1)
                    dve.wait_ge(s.inverted, m + 1)
                    if gates is not None:
                        dve.tensor_tensor(f, f, gates[:, i, :, b], ALU.mult).then_inc(s.factored, 1)
                        dve.wait_ge(s.factored, m + 1)
                    fb = f.unsqueeze(2).to_broadcast([P, H, HD])
                    here = y[:, i, :].rearrange("p (h d) -> p h d", h=H)
                    if b == 0:
                        dve.tensor_tensor(here, out[:, :, 0:HD], fb, ALU.mult).then_inc(s.written, 1)
                        return
                    dve.tensor_tensor(scaled[:, m % 2, :, :], out[:, :, 0:HD], fb, ALU.mult).then_inc(s.scaled_ready, 1)
                    dve.wait_ge(s.scaled_ready, (NB - 1) * i + b)
                    dve.wait_ge(s.written, m)
                    dve.tensor_tensor(here, here, scaled[:, m % 2, :, :], ALU.add).then_inc(s.written, 1)

                dve.wait_ge(s.parts_set, 1)
                maxima(0)
                place(0)
                for i in range(NT):
                    if i + 1 < NT:
                        maxima(i + 1)
                    for b in range(NB - 1):
                        write(i, b)
                    if i + 1 < NT:
                        place(i + 1)
                    write(i, NB - 1)


def sparse(nc, tag, proj, tab, w, ident, y):
    NG = T // CMP_STRIDE
    NK = NCMP + 1
    NB = 3
    with ExitStack() as c:
        sb = lambda n, shape, dt=F32: c.enter_context(nc.sbuf_tensor(f"{tag}_{n}", shape, dt))
        off = COL["nq"]
        q1, q2 = sb("q1", [P, H, T], F32R), sb("q2", [P, H, T], F32R)
        widths = [NK, T, T]
        k1, k2, k3 = ([sb(f"k{m}{b}", [P, widths[b]], F32R) for b in range(NB)] for m in (1, 2, 3))
        v = [sb("v0", [NK, HD + 1]), sb("v1", [P, NT, HD + 1]), sb("v2", [P, NT, HD + 1])]
        masks, mask_cmp = sb("masks", [P, 4, P], F32R), sb("mask_cmp", [P, NT, NK], F32R)
        mask_cmp_T = sb("mask_cmp_T", [NK, NT, P], F32R)
        identr, pick = sb("identr", [P, P], F32R), sb("pick", [NB * H, H, P])
        gates = sb("gates", [P, NT, H, 3])
        with ExitStack() as c1:
            sb1 = lambda n, shape: c1.enter_context(nc.sbuf_tensor(f"{tag}_{n}", shape, F32))
            ps1 = lambda n, shape: c1.enter_context(nc.psum_tensor(f"{tag}_{n}", shape, F32))
            raw = sb1("raw", [P, NT, D_IN - off])
            cols = lambda n: raw[:, :, COL[n] - off:COL[n] - off + SPLITS[n]]
            any_cmp = sb1("any_cmp", [P, NT])
            w1 = sb1("w1", [P, CMP_LEN // 2, CMP_HID])
            w2 = sb1("w2", [P, 2, 2, HD])
            pe_in, peT = sb1("pe_in", [CMP_LEN, P]), sb1("peT", [P, CMP_LEN])
            kvT = sb1("kvT", [P, T])
            u = sb1("u", [P, NG, CMP_STRIDE])
            th, hid = sb1("th", [P, 2, 2, NCMP]), sb1("hid", [P, 2, 2, NCMP])
            masks_in = sb1("masks_in", [P, 4, P])
            mask_cmp_in, mask_cmp_T_in = sb1("mask_cmp_in", [P, NT, NK]), sb1("mask_cmp_T_in", [NK, NT, P])
            qrows, krows = sb1("qrows", [2, H, NT]), sb1("krows", [HD, NB, T])
            pq, pk = ps1("pq", [HD, 2, H, P]), ps1("pk", [P, 2, 4, P])
            ph, pcmp = ps1("ph", [P, 2, 512]), ps1("pcmp", [HD, 2, 512])
            s = c1.enter_context(phase(nc, "raw_loaded", "loaded", "w1_loaded", "turned", "q_hi", "q_lo", "k_hi", "kv_copied",
                                       "k_lo", "pe_turned", "pe_copied", "placed", "q_turned", "tanh_ready", "hid_done",
                                       "cmp_ready", "cmp_hi", "gate_tanh", "gated", "zeroed", "half_read", "pool_step"))
            with nc.Block() as block:
                @block.sync
                def _(sp):
                    sp.dma_start(raw[:], tokens(proj, off, D_IN)).then_inc(s.raw_loaded, 16)
                    for i, n in enumerate("kv"):
                        sp.dma_start(pe_in[:, i * HD:(i + 1) * HD], w[f"cmp_pe_{n}"]).then_inc(s.loaded, 16)
                        sp.dma_start(w2[:, i, :, :], w[f"cmp_w2_{n}"].rearrange("(a p) d -> p a d", p=P)).then_inc(s.loaded, 16)
                    for dst, name in ((masks_in, "t_masks"), (mask_cmp_in, "t_mask_cmp"), (mask_cmp_T_in, "t_mask_cmp_T"),
                                      (qrows, "t_qrows"), (krows, "t_krows"), (pick, "t_pick"), (any_cmp, "t_any_cmp")):
                        sp.dma_start(dst[:], tab[name]).then_inc(s.loaded, 16)
                    for g0 in range(2):
                        if g0:
                            sp.wait_ge(s.half_read, 1)
                        for i, n in enumerate("kv"):
                            sp.dma_start(w1[i * HD:(i + 1) * HD, :, :],
                                         w[f"cmp_w1_{n}"].rearrange("(g j d) c -> g d j c", g=2, d=HD)[g0]).then_inc(s.w1_loaded, 16)

                @block.gpsimd
                def _(pool):
                    step = ordered(pool, s.pool_step)
                    step(pool.memset(q2[0:HD, :, :].bitcast(F32), 0.0))
                    for b in range(NB):
                        step(pool.memset(v[b][:], 1.0))
                    for k in (k1, k2):
                        step(pool.memset(k[0][:].bitcast(F32), 0.0))
                    pool.memset(k3[0][:].bitcast(F32), 0.0).then_inc(s.zeroed, 1)
                    pool.wait_ge(s.zeroed, 1)
                    pool.wait_ge(s.loaded, 176)
                    step(pool.tensor_copy(q2[32:34, :, :].rearrange("r h (t p) -> r h t p", p=P),
                                          qrows[:].unsqueeze(3).to_broadcast([2, H, NT, P])))
                    step(pool.tensor_copy(masks[:], masks_in[:]))
                    step(pool.tensor_copy(mask_cmp[:], mask_cmp_in[:]))
                    step(pool.tensor_copy(mask_cmp_T[:], mask_cmp_T_in[:]))
                    step(pool.tensor_copy(identr[:], ident[:]))
                    for b in range(NB):
                        for k in (k2, k3):
                            step(pool.tensor_copy(k[b][0:HD, :], krows[:, b, 0:widths[b]]))
                    for n in range(2):
                        pool.wait_ge(s.k_hi, 2 * (n + 1))
                        for k in (k1, k3):
                            step(pool.tensor_copy(k[1 + n][HD:P, :], k1[1 + n][0:HD, :]))
                    pool.wait_ge(s.q_hi, NT)
                    step(pool.tensor_copy(q2[HD:P, :, :], q1[0:HD, :, :]))
                    pool.wait_ge(s.cmp_hi, 1)
                    for k in (k1, k3):
                        step(pool.tensor_copy(k[0][HD:P, :], k1[0][0:HD, :]))

                @block.tensor
                def _(pe):
                    pe.wait_ge(s.loaded, 176)
                    pe.wait_ge(s.raw_loaded, 16)
                    pe.transpose(ph[:, 0, 0:CMP_LEN], pe_in[:], ident[0:CMP_LEN, 0:CMP_LEN]).then_inc(s.pe_turned, 1)
                    n = 0
                    for part in ("kc", "ks", "kw"):
                        for half in range(2):
                            if n >= 2:
                                pe.wait_ge(s.kv_copied, n - 1)
                            for j in range(4):
                                t = 4 * half + j
                                if part == "kc":
                                    src, dst = raw[:, t, COL["kc"] - off:COL["ks"] - off], pk[:, n % 2, j, :]
                                else:
                                    src, dst = cols(part)[:, t, :], pk[0:HD, n % 2, j, :]
                                mm = pe.transpose(dst, src, ident[:])
                            mm.then_inc(s.turned, 1)
                            n += 1
                    pe.wait_ge(s.pe_copied, 1)
                    for g0 in range(2):
                        pe.wait_ge(s.w1_loaded, 32 * g0 + 32)
                        pe.wait_ge(s.placed, g0 + 1)
                        for j in range(CMP_STRIDE):
                            for a in range(2):
                                for i in range(2):
                                    half = slice(i * HD, (i + 1) * HD)
                                    mm = pe.matmul(ph[:, i, a * 64:a * 64 + NCMP], w1[half, j, a * P:(a + 1) * P],
                                                   u[half, g0:g0 + NCMP, j], start=(g0 == 0 and j == 0 and a == 0),
                                                   stop=(g0 == 1 and j == CMP_STRIDE - 1), skip_group_check=True)
                        mm.then_inc(s.half_read, 1)
                    for t in range(NT):
                        if t >= 2:
                            pe.wait_ge(s.q_lo, t - 1)
                        for h in range(H):
                            mm = pe.transpose(pq[:, t % 2, h, :], raw[:, t, h * HD:(h + 1) * HD], ident[:])
                        mm.then_inc(s.q_turned, 1)
                    pe.wait_ge(s.hid_done, 2)
                    for a in range(2):
                        pe.matmul(pcmp[:, 0, 0:NCMP], w2[:, 0, a, :], hid[:, 0, a, :], start=(a == 0), stop=(a == 1))
                    for a in range(2):
                        mm = pe.matmul(pcmp[0:NCMP, 1, 0:HD], hid[:, 1, a, :], w2[:, 1, a, :], start=(a == 0), stop=(a == 1))
                    mm.then_inc(s.cmp_ready, 1)

                @block.scalar
                def _(act):
                    act.wait_ge(s.raw_loaded, 16)
                    act.activation(gates[:].rearrange("p t h b -> p t (h b)"), cols("gate"), ACT.Tanh, scale=0.5).then_inc(s.gate_tanh, 1)
                    for n in range(4):
                        act.wait_ge(s.turned, n + 3)
                        act.activation(k1[1 + n // 2][0:HD, (n % 2) * 512:(n % 2 + 1) * 512],
                                       pk[0:HD, n % 2, :, :].rearrange("p a b -> p (a b)"), ACT.Copy).then_inc(s.k_lo, 1)
                    act.wait_ge(s.half_read, 2)
                    for i in range(2):
                        act.activation(th[:, i, :, :], ph[:, i, 0:P].rearrange("p (a n) -> p a n", a=2)[:, :, 0:NCMP], ACT.Tanh,
                                       scale=0.5).then_inc(s.tanh_ready, 1)
                    for t in range(NT):
                        act.wait_ge(s.q_turned, t + 1)
                        act.activation(q1[0:HD, :, t * P:(t + 1) * P], pq[:, t % 2, :, :], ACT.Copy, scale=float(HD ** -0.5)).then_inc(s.q_hi, 1)
                    act.wait_ge(s.cmp_ready, 1)
                    act.wait_ge(s.zeroed, 1)
                    act.activation(k1[0][0:HD, 0:NCMP], pcmp[:, 0, 0:NCMP], ACT.Copy, scale=0.5).then_inc(s.cmp_hi, 1)
                    act.activation(v[0][0:NCMP, 0:HD], pcmp[0:NCMP, 1, 0:HD], ACT.Copy, scale=0.5)

                @block.vector
                def _(dve):
                    dve.wait_ge(s.pe_turned, 1)
                    dve.tensor_copy(peT[:], ph[:, 0, 0:CMP_LEN]).then_inc(s.pe_copied, 1)
                    for n in range(2):
                        dve.wait_ge(s.turned, n + 1)
                        dve.tensor_copy(kvT[:, n * 512:(n + 1) * 512], pk[:, n, :, :].rearrange("p a b -> p (a b)")).then_inc(s.kv_copied, 1)
                    dve.wait_ge(s.pe_copied, 1)
                    dve.wait_ge(s.kv_copied, 2)
                    for g0 in range(2):
                        if g0:
                            dve.wait_ge(s.half_read, 1)
                        dve.tensor_tensor(u[:], kvT[:].rearrange("p (n j) -> p n j", j=CMP_STRIDE),
                                          peT[:, g0 * CMP_STRIDE:(g0 + 1) * CMP_STRIDE].unsqueeze(1).to_broadcast([P, NG, CMP_STRIDE]),
                                          ALU.add).then_inc(s.placed, 1)
                        if g0 == 0:
                            for n in range(4):
                                b, here = 1 + n // 2, slice((n % 2) * 512, (n % 2 + 1) * 512)
                                dve.wait_ge(s.k_lo, n + 1)
                                dve.tensor_tensor(k2[b][HD:P, here], pk[0:HD, n % 2, :, :].rearrange("p a b -> p (a b)"),
                                                  k1[b][0:HD, here].bitcast(F32), ALU.subtract).then_inc(s.kv_copied, 1)
                                dve.sem_inc(s.k_hi, 1)
                    dve.wait_ge(s.zeroed, 1)
                    for b, part in ((1, "vs"), (2, "vw")):
                        dve.tensor_copy(v[b][:, :, 0:HD], cols(part))
                    dve.wait_ge(s.gate_tanh, 1)
                    dve.tensor_scalar(gates[:], gates[:], 0.5, 0.5, ALU.mult, ALU.add).then_inc(s.gated, 1)
                    dve.wait_ge(s.gated, 1)
                    dve.wait_ge(s.loaded, 176)
                    dve.tensor_tensor(gates[:, :, :, 0], gates[:, :, :, 0], any_cmp[:].unsqueeze(2).to_broadcast([P, NT, H]), ALU.mult)
                    dve.wait_ge(s.tanh_ready, 2)
                    for i in range(2):
                        dve.scalar_tensor_tensor(hid[:, i, :, :], th[:, i, :, :], 1.0,
                                                 ph[:, i, 0:P].rearrange("p (a n) -> p a n", a=2)[:, :, 0:NCMP],
                                                 ALU.add, ALU.mult).then_inc(s.hid_done, 1)
                    for t in range(NT):
                        here = slice(t * P, (t + 1) * P)
                        dve.wait_ge(s.q_hi, t + 1)
                        dve.scalar_tensor_tensor(q1[HD:P, :, here], pq[:, t % 2, :, :], HD ** -0.5, q1[0:HD, :, here].bitcast(F32),
                                                 ALU.mult, ALU.subtract).then_inc(s.q_lo, 1)
                    dve.wait_ge(s.cmp_hi, 1)
                    dve.scalar_tensor_tensor(k2[0][HD:P, 0:NCMP], pcmp[:, 0, 0:NCMP], 0.5, k1[0][0:HD, 0:NCMP].bitcast(F32),
                                             ALU.mult, ALU.subtract)

        def branch(b, width, tiles, mask, mask_T):
            def score(i, h, a, z):
                return q2[:, h, i * P:(i + 1) * P], k3[b][:, a * width:(z + 1) * width]

            def score_T(i, kt, out):
                here, keys = slice(i * P, (i + 1) * P), slice(kt * width, (kt + 1) * width)
                return [(out, k2[b][:, keys], q2[:, :, here], True, False),
                        (out, k1[b][:, keys], q1[:, :, here], False, True)]

            values = (lambda kt, h: v[0][:]) if b == 0 else (lambda kt, h: v[b][:, kt, :])
            return Branch(width, tiles, score, mask, score_T, mask_T, values, identr,
                          lambda i: q2[0:NB * H, :, i * P:(i + 1) * P])

        DIAG, DIAG_T, FAR, FAR_T = (masks[:, n, :] for n in range(4))
        reach = WIN // P
        branches = [
            branch(0, NK, lambda i: [0], lambda i, kt: mask_cmp[:, i, :], lambda i, kt: mask_cmp_T[:, i, :]),
            branch(1, P, lambda i: list(range(i + 1)), lambda i, kt: DIAG if kt == i else None,
                   lambda i, kt: DIAG_T if kt == i else None),
            branch(2, P, lambda i: list(range(max(0, i - reach), i + 1)),
                   lambda i, kt: DIAG if kt == i else FAR if kt == i - reach else None,
                   lambda i, kt: DIAG_T if kt == i else FAR_T if kt == i - reach else None),
        ]
        attend(nc, tag, y, branches, ident, pick[:], gates)


def hybrid_layers(nc, a, tab, out):
    proj = nc.dram_tensor("projections", (T, D_IN), F32).ap()
    with ExitStack() as c:
        h = c.enter_context(nc.sbuf_tensor("h", [P, NT, D], F32))
        ident = c.enter_context(nc.sbuf_tensor("ident", [P, P], F32))
        with phase(nc, "x_loaded") as s, nc.Block() as block:
            @block.sync
            def _(sp):
                sp.dma_start(h[:], tokens(a["x"][0], 0, D)).then_inc(s.x_loaded, 16)
                sp.dma_start(ident[:], tab["t_ident"]).then_inc(s.x_loaded, 16)
                sp.wait_ge(s.x_loaded, 32)
        layer_norm(nc, "norm_emb", h, a["ln_emb_g"], a["ln_emb_b"])
        with nc.Fori(0, DEPTH) as l:
            w = {n: a[n][l] for n in a if n not in ("x", "ln_emb_g", "ln_emb_b")}
            with ExitStack() as c1:
                hi, lo = (c1.enter_context(nc.sbuf_tensor(n, [P, KT, T], F32R)) for n in ("x_hi", "x_lo"))
                feature_major(nc, "fmx", h, hi, lo, ident)
                project(nc, "in", w["w_in"], D_IN, hi, lo, to_dram=proj)
            with ExitStack() as c1:
                y = c1.enter_context(nc.sbuf_tensor("y", [P, NT, D], F32))
                ssd(nc, "ssd", proj, tab, w, ident, y[:, :, 0:GW])
                latent(nc, "mla", proj, tab, w, ident, y[:, :, GW:2 * GW])
                retention(nc, "ret", proj, tab, ident, y[:, :, 2 * GW:3 * GW])
                sparse(nc, "nsa", proj, tab, w, ident, y[:, :, 3 * GW:4 * GW])
                hi, lo = (c1.enter_context(nc.sbuf_tensor(n, [P, KT, T], F32R)) for n in ("y_hi", "y_lo"))
                feature_major(nc, "fmy", y, hi, lo, ident)
                project(nc, "out", w["w_out"], D, hi, lo, into=h)
            layer_norm(nc, "norm1", h, w["ln1_g"], w["ln1_b"])
            with ExitStack() as c1:
                hi, lo = (c1.enter_context(nc.sbuf_tensor(n, [P, KT, T], F32R)) for n in ("h_hi", "h_lo"))
                feature_major(nc, "fmh", h, hi, lo, ident)
                mlp(nc, w["w_mlp1"], w["w_mlp2"], hi, lo, h)
            layer_norm(nc, "norm2", h, w["ln2_g"], w["ln2_b"])
        with phase(nc, "stored") as s, nc.Block() as block:
            @block.sync
            def _(sp):
                sp.dma_start(tokens(out[0], 0, D), h[:]).then_inc(s.stored, 16)
                sp.wait_ge(s.stored, 16)


_INS = ["x", "ln_emb_g", "ln_emb_b", "w_in", "conv_w", "conv_b", "dt_bias", "a_log", "d_skip", "ssm_norm_g",
        "q_norm_g", "w_uq", "kv_norm_g", "w_ukv", "cmp_pe_k", "cmp_w1_k", "cmp_w2_k", "cmp_pe_v", "cmp_w1_v",
        "cmp_w2_v", "w_out", "ln1_g", "ln1_b", "w_mlp1", "w_mlp2", "ln2_g", "ln2_b"]


def kernel(**inputs):
    import concourse.bacc as bacc
    from concourse.bass_utils import run_bass_kernel_spmd

    nc = bacc.Bacc("TRN2", target_bir_lowering=False, num_devices=1)
    arrays = {n: np.ascontiguousarray(inputs[n]) for n in _INS}
    tables = shape_tables()
    dram = {n: nc.dram_tensor(n, v.shape, F32, kind="ExternalInput").ap() for n, v in (arrays | tables).items()}
    out = nc.dram_tensor("out", (1, T, D), F32, kind="ExternalOutput").ap()
    hybrid_layers(nc, {n: dram[n] for n in arrays}, {n: dram[n] for n in tables}, out)
    r = run_bass_kernel_spmd(nc, [arrays | tables], core_ids=[0])
    return r.results[0]["out"]
```
